# Optimizing a Trainium2 kernel written in Bass

```python
import jax, jax.numpy as jnp
from jax import lax
import numpy as np

D_MODEL = 2048
BATCH = 1
SEQ = 512
DEPTH = 1
DEC_BATCH = 1
DEC_SEQ = 64
PAST_LEN = 512

CHUNK = 64
HEAD_DIM = 64
N_HEADS_A = D_MODEL // (2 * HEAD_DIM)
N_KV_A = max(1, N_HEADS_A // 8)
Q_PER_KV = N_HEADS_A // N_KV_A
N_HEADS_B = D_MODEL // (2 * HEAD_DIM)
WINDOW = 128
WIN_CHUNKS = WINDOW // CHUNK
ROPE_THETA = 10000.0
D_FF = 4 * D_MODEL
D_PLE = 256
Q_BLOCK = 128
LN_EPS = 1e-5
ATTN_SCALE = HEAD_DIM ** -0.5
D_A = N_HEADS_A * HEAD_DIM
D_KV_A = N_KV_A * HEAD_DIM
D_B = N_HEADS_B * HEAD_DIM
D_MIX = D_A + D_B
D_IN = D_A + 2 * D_KV_A + 3 * D_B + N_HEADS_B
SPLITS = (D_A, D_A + D_KV_A, D_A + 2 * D_KV_A, D_A + 2 * D_KV_A + D_B,
          D_A + 2 * D_KV_A + 2 * D_B, D_A + 2 * D_KV_A + 3 * D_B)
DEEPNORM_ALPHA = (2.0 * DEPTH) ** 0.25
DEEPNORM_BETA = (8.0 * DEPTH) ** -0.25

kernel_name = "hybrid_swa_sink_fox_stream_step"

def layer_norm(x, g, b):
    xf = x.astype(jnp.float32)
    mu = jnp.mean(xf, axis=-1, keepdims=True)
    var = jnp.mean(jnp.square(xf - mu), axis=-1, keepdims=True)
    y = (xf - mu) * lax.rsqrt(var + LN_EPS) * g.astype(jnp.float32) + b.astype(jnp.float32)
    return y.astype(x.dtype)

def rope(x, pos):
    half = HEAD_DIM // 2
    inv = ROPE_THETA ** (-jnp.arange(half, dtype=jnp.float32) / half)
    ang = pos.astype(jnp.float32)[:, None] * inv[None, :]
    cos = jnp.cos(ang)[None, :, None, :]
    sin = jnp.sin(ang)[None, :, None, :]
    xf = x.astype(jnp.float32)
    x1, x2 = xf[..., :half], xf[..., half:]
    return jnp.concatenate([x1 * cos - x2 * sin, x2 * cos + x1 * sin], axis=-1).astype(x.dtype)

def mixer_inputs(h, w_in, b_f):
    B, S, _ = h.shape
    z = h @ w_in
    qa, ka, va, qb, kb, vb, fz = jnp.split(z, SPLITS, axis=-1)
    qa = qa.reshape(B, S, N_HEADS_A, HEAD_DIM)
    ka = ka.reshape(B, S, N_KV_A, HEAD_DIM)
    va = va.reshape(B, S, N_KV_A, HEAD_DIM)
    qb = qb.reshape(B, S, N_HEADS_B, HEAD_DIM)
    kb = kb.reshape(B, S, N_HEADS_B, HEAD_DIM)
    vb = vb.reshape(B, S, N_HEADS_B, HEAD_DIM)
    logf = jax.nn.log_sigmoid(fz.astype(jnp.float32) + b_f.astype(jnp.float32))
    return qa, ka, va, qb, kb, vb, logf

def sink_attention(q, k, v, mask, sinks):
    s = jnp.einsum("bnqhgd,bnkhd->bnhgqk", q, k, preferred_element_type=jnp.float32) * ATTN_SCALE
    if mask is not None:
        s = jnp.where(mask[:, :, None, None], s, -jnp.inf)
    sink = sinks.astype(jnp.float32).reshape(1, 1, N_KV_A, Q_PER_KV, 1, 1)
    m = jnp.maximum(jnp.max(s, axis=-1, keepdims=True), sink)
    e = jnp.exp(s - m)
    p = e / (jnp.sum(e, axis=-1, keepdims=True) + jnp.exp(sink - m))
    return jnp.einsum("bnhgqk,bnkhd->bnqhgd", p.astype(v.dtype), v)

def swa_prompt(q, k, v, sinks):
    B, S = q.shape[:2]
    nc = S // CHUNK
    nk = WIN_CHUNKS + 1
    pad = ((0, 0), (WIN_CHUNKS * CHUNK, 0), (0, 0), (0, 0))
    kc = jnp.pad(k, pad).reshape(B, nc + WIN_CHUNKS, CHUNK, N_KV_A, HEAD_DIM)
    vc = jnp.pad(v, pad).reshape(B, nc + WIN_CHUNKS, CHUNK, N_KV_A, HEAD_DIM)
    kband = jnp.concatenate([kc[:, j:j + nc] for j in range(nk)], axis=2)
    vband = jnp.concatenate([vc[:, j:j + nc] for j in range(nk)], axis=2)
    key_chunk = jnp.arange(nc)[:, None] + jnp.arange(nk)[None, :] - WIN_CHUNKS
    valid = jnp.repeat(key_chunk >= 0, CHUNK, axis=1)[None, :, None, :]
    qg = q.reshape(B, nc, CHUNK, N_KV_A, Q_PER_KV, HEAD_DIM)
    o = sink_attention(qg, kband, vband, valid, sinks)
    return o.reshape(B, S, D_A)

def swa_sample(q, k_all, v_all, sinks):
    B, T = q.shape[:2]
    qg = q.reshape(B, 1, T, N_KV_A, Q_PER_KV, HEAD_DIM)
    o = sink_attention(qg, k_all[:, None], v_all[:, None], None, sinks)
    return o.reshape(B, T, D_A)

def fox_attention(q, k, v, f_q, f_k, pos_q, pos_k):
    s = jnp.einsum("bqhd,bkhd->bhqk", q, k, preferred_element_type=jnp.float32) * ATTN_SCALE
    s = s + jnp.swapaxes(f_q, 1, 2)[..., :, None] - jnp.swapaxes(f_k, 1, 2)[..., None, :]
    s = jnp.where(pos_k[None, :] <= pos_q[:, None], s, -jnp.inf)
    p = jax.nn.softmax(s, axis=-1)
    return jnp.einsum("bhqk,bkhd->bqhd", p.astype(v.dtype), v)

def fox_prompt(q, k, v, logf):
    B, S = q.shape[:2]
    F = jnp.cumsum(logf, axis=1)
    nb = S // Q_BLOCK
    pos = jnp.arange(S, dtype=jnp.int32)
    qs = jnp.swapaxes(q.reshape(B, nb, Q_BLOCK, N_HEADS_B, HEAD_DIM), 0, 1)
    fs = jnp.swapaxes(F.reshape(B, nb, Q_BLOCK, N_HEADS_B), 0, 1)
    ps = pos.reshape(nb, Q_BLOCK)
    out = lax.map(lambda a: fox_attention(a[0], k, v, a[1], F, a[2], pos), (qs, fs, ps))
    return jnp.swapaxes(out, 0, 1).reshape(B, S, D_B)

def finish_layer(h, mix, pe, w_o, ln1_g, ln1_b, w_up, w_down, ln2_g, ln2_b, w_pg, b_pg, w_pe):
    h = layer_norm(DEEPNORM_ALPHA * h + mix @ w_o, ln1_g, ln1_b)
    hidden = jnp.square(jax.nn.relu(h @ w_up))
    h = layer_norm(DEEPNORM_ALPHA * h + hidden @ w_down, ln2_g, ln2_b)
    return h + jax.nn.sigmoid(h @ w_pg + b_pg) * (pe @ w_pe)

def setup_inputs(seed: int = 0) -> dict:
    key = jax.random.key(seed)
    ks = jax.random.split(key, 24)
    n = jax.random.normal
    f32 = jnp.float32
    swa_len = min(WINDOW, PAST_LEN)
    return {
        "x_prompt": n(ks[0], (BATCH, SEQ, D_MODEL), f32),
        "x_sample": n(ks[1], (DEC_BATCH, DEC_SEQ, D_MODEL), f32),
        "p_prompt": n(ks[2], (DEPTH, BATCH, SEQ, D_PLE), f32),
        "p_sample": n(ks[3], (DEPTH, DEC_BATCH, DEC_SEQ, D_PLE), f32),
        "cache_swa_k": n(ks[4], (DEPTH, DEC_BATCH, swa_len, N_KV_A, HEAD_DIM), f32),
        "cache_swa_v": n(ks[5], (DEPTH, DEC_BATCH, swa_len, N_KV_A, HEAD_DIM), f32),
        "cache_fox_k": n(ks[6], (DEPTH, DEC_BATCH, PAST_LEN, N_HEADS_B, HEAD_DIM), f32),
        "cache_fox_v": n(ks[7], (DEPTH, DEC_BATCH, PAST_LEN, N_HEADS_B, HEAD_DIM), f32),
        "cache_fox_logf": jax.nn.log_sigmoid(3.0 + n(ks[8], (DEPTH, DEC_BATCH, PAST_LEN, N_HEADS_B), f32)),
        "ln0_g": 1.0 + 0.02 * n(ks[9], (D_MODEL,), f32),
        "ln0_b": 0.02 * n(ks[10], (D_MODEL,), f32),
        "w_in": n(ks[11], (DEPTH, D_MODEL, D_IN), f32) * D_MODEL ** -0.5,
        "b_f": 3.0 + 0.5 * n(ks[12], (DEPTH, N_HEADS_B), f32),
        "sinks": n(ks[13], (DEPTH, N_HEADS_A), f32),
        "w_o": n(ks[14], (DEPTH, D_MIX, D_MODEL), f32) * (D_MIX ** -0.5 * DEEPNORM_BETA),
        "ln1_g": 1.0 + 0.02 * n(ks[15], (DEPTH, D_MODEL), f32),
        "ln1_b": 0.02 * n(ks[16], (DEPTH, D_MODEL), f32),
        "w_up": n(ks[17], (DEPTH, D_MODEL, D_FF), f32) * D_MODEL ** -0.5,
        "w_down": n(ks[18], (DEPTH, D_FF, D_MODEL), f32) * (D_FF ** -0.5 * DEEPNORM_BETA),
        "ln2_g": 1.0 + 0.02 * n(ks[19], (DEPTH, D_MODEL), f32),
        "ln2_b": 0.02 * n(ks[20], (DEPTH, D_MODEL), f32),
        "w_pg": n(ks[21], (DEPTH, D_MODEL, D_MODEL), f32) * D_MODEL ** -0.5,
        "b_pg": 0.02 * n(ks[22], (DEPTH, D_MODEL), f32),
        "w_pe": n(ks[23], (DEPTH, D_PLE, D_MODEL), f32) * D_PLE ** -0.5,
    }

def reference(x_prompt, x_sample, p_prompt, p_sample, cache_swa_k, cache_swa_v, cache_fox_k, cache_fox_v,
              cache_fox_logf, ln0_g, ln0_b, w_in, b_f, sinks, w_o, ln1_g, ln1_b, w_up, w_down, ln2_g, ln2_b,
              w_pg, b_pg, w_pe):
    S = x_prompt.shape[1]
    T = x_sample.shape[1]
    past = cache_fox_k.shape[2]
    pos_p = jnp.arange(S, dtype=jnp.int32)
    pos_s = past + jnp.arange(T, dtype=jnp.int32)
    keep_p = min(WINDOW, S)
    hp = layer_norm(x_prompt, ln0_g, ln0_b)
    hs = layer_norm(x_sample, ln0_g, ln0_b)
    swa_kp, swa_vp, fox_kp, fox_vp, fox_fp = [], [], [], [], []
    swa_ks, swa_vs, fox_ks, fox_vs, fox_fs = [], [], [], [], []
    for i in range(DEPTH):
        qa, ka, va, qb, kb, vb, logf = mixer_inputs(hp, w_in[i], b_f[i])
        qa = rope(qa, pos_p)
        ka = rope(ka, pos_p)
        oa = swa_prompt(qa, ka, va, sinks[i])
        ob = fox_prompt(qb, kb, vb, logf)
        swa_kp.append(ka[:, S - keep_p:])
        swa_vp.append(va[:, S - keep_p:])
        fox_kp.append(kb)
        fox_vp.append(vb)
        fox_fp.append(logf)
        hp = finish_layer(hp, jnp.concatenate([oa, ob], axis=-1), p_prompt[i], w_o[i], ln1_g[i], ln1_b[i],
                          w_up[i], w_down[i], ln2_g[i], ln2_b[i], w_pg[i], b_pg[i], w_pe[i])
        qa, ka, va, qb, kb, vb, logf = mixer_inputs(hs, w_in[i], b_f[i])
        qa = rope(qa, pos_s)
        ka = rope(ka, pos_s)
        k_all = jnp.concatenate([cache_swa_k[i].astype(ka.dtype), ka], axis=1)
        v_all = jnp.concatenate([cache_swa_v[i].astype(va.dtype), va], axis=1)
        oa = swa_sample(qa, k_all, v_all, sinks[i])
        win = cache_swa_k.shape[2]
        swa_ks.append(k_all[:, k_all.shape[1] - win:])
        swa_vs.append(v_all[:, v_all.shape[1] - win:])
        kf = jnp.concatenate([cache_fox_k[i].astype(kb.dtype), kb], axis=1)
        vf = jnp.concatenate([cache_fox_v[i].astype(vb.dtype), vb], axis=1)
        F_all = jnp.cumsum(jnp.concatenate([cache_fox_logf[i].astype(jnp.float32), logf], axis=1), axis=1)
        pos_k = jnp.arange(past + T, dtype=jnp.int32)
        ob = fox_attention(qb, kf, vf, F_all[:, past:], F_all, pos_s, pos_k).reshape(hs.shape[0], T, D_B)
        fox_ks.append(kb)
        fox_vs.append(vb)
        fox_fs.append(logf)
        hs = finish_layer(hs, jnp.concatenate([oa, ob], axis=-1), p_sample[i], w_o[i], ln1_g[i], ln1_b[i],
                          w_up[i], w_down[i], ln2_g[i], ln2_b[i], w_pg[i], b_pg[i], w_pe[i])
    return (hp, hs,
            jnp.stack(swa_kp), jnp.stack(swa_vp), jnp.stack(fox_kp), jnp.stack(fox_vp), jnp.stack(fox_fp),
            jnp.stack(swa_ks), jnp.stack(swa_vs), jnp.stack(fox_ks), jnp.stack(fox_vs), jnp.stack(fox_fs))


_drawn_inputs = setup_inputs


def setup_inputs(seed=0):
    import zlib

    import numpy as np

    out = dict(_drawn_inputs(seed))
    spreads = {}
    factors = {'cache_fox_logf': 64.0,
     'ln0_g': 2.766,
     'sinks': 44.536,
     'ln1_g': 2.931,
     'ln1_b': 3.098,
     'ln2_g': 9.548,
     'ln2_b': 9.408,
     'b_pg': 64.0,
     'cache_fox_k': 3.13,
     'cache_fox_v': 4.035,
     'ln0_b': 4.527}
    for name, (base, spread) in spreads.items():
        noise = np.random.default_rng([zlib.crc32(name.encode()), seed]).standard_normal(out[name].shape)
        drawn = base * np.exp(spread * noise) if base else spread * noise
        out[name] = __import__('jax').numpy.asarray(drawn.astype(out[name].dtype))
    for name, factor in factors.items():
        out[name] = (out[name] * factor).astype(out[name].dtype)
    return out
```

```python
import concourse.bass as bass
from concourse import mybir
from contextlib import ExitStack

D = 2048
PROMPT, SAMPLE = 512, 64
TOK = PROMPT + SAMPLE
HALF = TOK // 2
KT = D // 128
PAST = 512
WIN = 128
PAIRS = 8
FF_BLOCKS = 16
EPS = 1e-5
ALPHA = 2.0 ** 0.25
SCALE = 0.125
NEG = -(2.0 ** 100)

RING = 4
U_KV = 0
U_QA = U_KV + 4
U_FOX = U_QA + 2 * PAIRS
U_O = U_FOX + 6 * PAIRS
U_MLP = U_O + 2 * KT
U_PE = U_MLP + 16 * FF_BLOCKS
U_PG = U_PE + 4
UNITS = U_PG + 2 * KT

T_KV = 0
T_QA = T_KV + 3
T_FOX = T_QA + PAIRS
T_O = T_FOX + 3 * PAIRS
T_MLP = T_O + KT
T_PE = T_MLP + 20 * FF_BLOCKS
T_PG = T_PE + KT

STEPS = 10
SLOTS = STEPS + 3
SWA_SLOTS = {c: ([c - 4] if c < 15 else [11, 12]) for c in range(4, 16)}
FOX_SLOTS = {4 + 3 * j: [j] for j in range(SLOTS)}
F_X, F_M, F_E, F_W, F_L, F_D, F_R, F_G = (TOK * k for k in range(8))
F_SUM = F_G + TOK
F_ALL = TOK + PAST
F_HI = F_X
F_LO = F_HI + F_ALL
F_NHI = F_LO + F_ALL
F_NLO = F_SUM + F_ALL
F_C = F_NLO + F_ALL
F_ONE = F_C + PAST
N_CONSTS = 13
CACHE_COL = TOK
P_COLS = 640


def lin(const, i, step):
    return const if i is None else i * step + const


class Chain:

    def __init__(self, eng, sem):
        self.eng, self.sem, self.n, self.i, self.step, self.start = eng, sem, 0, None, 0, 0

    def add(self, ins):
        ins.then_inc(self.sem, 1)
        self.n += 1
        return ins

    def wait(self, back=0):
        self.eng.wait_ge(self.sem, lin(self.n - back, self.i, self.step))

    def enter(self, i, step):
        self.i, self.step, self.start = i, step, self.n

    def leave(self, count):
        assert self.n - self.start == self.step, (self.n - self.start, self.step)
        self.n, self.i = self.start + self.step * count, None


class Ahead:

    def __init__(self, split):
        self.split, self.next = split, 0

    def upto(self, u, i=None, du=0):
        while self.next <= min(u, UNITS - 1):
            self.split(self.next, i, du)
            self.next += 1

    def leave(self, count, du):
        self.next += du * (count - 1)


def feature_tile(tensor, kt):
    if isinstance(kt, int):
        return tensor[:, kt, :]
    return tensor[:, bass.ds(kt, 1), :].rearrange("p o t -> p (o t)")


def halves(ap):
    return ap.rearrange("p (a b) -> p a b", a=2)


def freed(n):
    return n % 2, n // 2 + 2


def step_of(s):
    return (s // 4, s % 4) if s < 8 else (s - 8, 4)



def span(kind, j):
    head, qt = step_of(j)
    if kind == "swa":
        return 512 * (j % 2), 1 + (128 if qt == 0 else 256 if qt < 4 else WIN + SAMPLE)
    return (512 * (j % 2), 128 * (qt + 1)) if qt < 4 else (0, PAST + SAMPLE)


def turn_width(kind, qt):
    if kind == "swa":
        return 128 if qt == 0 else 256 if qt < 4 else 128
    return 128 * (qt + 1) if qt < 4 else 5 * SAMPLE


def build(nc, t):
    f32, f32r = mybir.dt.float32, mybir.dt.float32r
    ACT, ALU = mybir.ActivationFunctionType, mybir.AluOpType
    AX = mybir.AxisListType.X
    outer = ExitStack()
    with outer:
        def sb(name, shape, dt=f32, scope=outer):
            return scope.enter_context(nc.sbuf_tensor(name, shape, dt))

        def sem(name):
            return outer.enter_context(nc.semaphore(name))

        x_hi = sb("x_hi", [128, KT, TOK], f32r)
        x_lo = sb("x_lo", [128, KT, TOK], f32r)
        acc = sb("acc", [128, KT, TOK])
        w_raw = sb("w_raw", [128, RING, 1024])
        w_hi = sb("w_hi", [128, RING, 1024], f32r)
        w_lo = sb("w_lo", [128, RING, 1024], f32r)
        ident = sb("ident", [128, 128])
        ident_r = sb("ident_r", [128, 128], f32r)
        tri_r = sb("tri_r", [128, 128], f32r)
        mean_w = sb("mean_w", [128, 128])
        cols = sb("cols", [128, 7 * KT])
        stat = sb("stat", [128, 3, 3])
        eps = sb("eps", [128, 1])
        st = sb("st", [128, 5, TOK])
        S1, S2, SH, WK = (st[:, k, :] for k in range(4))
        WK2 = st[:, 4, :]
        MU, VAR, RSTD = S1, S2, SH

        swa = ExitStack()
        cos_t = sb("cos_t", [128, TOK], f32, swa)
        sin_t = sb("sin_t", [128, TOK], f32, swa)
        swap = sb("swap", [128, 128], f32, swa)
        win_r = sb("win_r", [128, 256], f32r, swa)
        win_f = sb("win_f", [128, 256], f32, swa)
        tri_f = sb("tri_f", [128, 128], f32, swa)
        sinks = sb("sinks", [128, 2 * PAIRS], f32, swa)
        wf = sb("wf", [128, 256], f32, swa)
        wf_hi = sb("wf_hi", [128, 256], f32r, swa)
        wf_lo = sb("wf_lo", [128, 256], f32r, swa)
        bf = sb("bf", [16, 1], f32, swa)
        sk1 = sb("sk1", [128, 2, TOK + WIN], f32r, swa)
        sk2 = sb("sk2", [128, 2, TOK + WIN], f32r, swa)
        sq1 = sb("sq1", [128, 2, TOK], f32r, swa)
        z_t = sb("z_t", [128, TOK], f32, swa)
        rot = sb("rot", [128, TOK], f32, swa)
        rot2 = sb("rot2", [128, TOK], f32, swa)
        va_t = sb("va_t", [128, TOK], f32, swa)
        ck_t = sb("ck_t", [128, WIN], f32, swa)
        cv_t = sb("cv_t", [128, WIN], f32, swa)
        sv = sb("sv", [128, 6, 128], f32, swa)
        s_p = sb("s_p", [128, 3, 2 * 128 + 1], f32, swa)
        s_pt = sb("s_pt", [128, 2, 512], f32, swa)
        swa.close()

        fox = ExitStack()
        fq1 = sb("fq1", [128, 2, TOK], f32r, fox)
        fq2 = sb("fq2", [128, 2, TOK], f32r, fox)
        fk1 = sb("fk1", [128, 2, TOK], f32r, fox)
        fk2 = sb("fk2", [128, 2, TOK], f32r, fox)
        fc1 = sb("fc1", [128, 2, PAST], f32r, fox)
        fc2 = sb("fc2", [128, 2, PAST], f32r, fox)
        v_t = sb("v_t", [128, TOK], f32, fox)
        k_t = sb("k_t", [128, TOK], f32, fox)
        fv = sb("fv", [128, 5, 128], f32, fox)
        c_t = sb("c_t", [128, PAST], f32, fox)
        c_v = sb("c_v", [128, 4, 128], f32, fox)
        f_p = sb("f_p", [128, 3, P_COLS], f32, fox)
        f_pt = sb("f_pt", [128, 2, 512], f32, fox)
        fox.close()

        wo = ExitStack()
        y = sb("y", [128, KT, TOK], f32, wo)
        wo.close()

        late = ExitStack()
        p_raw = sb("p_raw", [128, 2, TOK], f32, late)
        p_hi = sb("p_hi", [128, 2, TOK], f32r, late)
        p_lo = sb("p_lo", [128, 2, TOK], f32r, late)
        mlp = ExitStack()
        hid_hi = sb("hid_hi", [128, 2, 4, TOK], f32r, mlp)
        hid_lo = sb("hid_lo", [128, 2, 4, TOK], f32r, mlp)
        mlp.close()
        pe_out = sb("pe_out", [128, KT, TOK], f32, late)
        late.close()

        tiles_ps = [outer.enter_context(nc.psum_tensor(f"tile{k}", [128, 2, 512], f32)) for k in range(2)]
        misc = outer.enter_context(nc.psum_tensor("misc", [128, 2048], f32))
        scores_ps, turn_ps, out_ps = misc[:, 0:1024], misc[:, 1024:1536], misc[:, 1536:2048]

        def tile_ps(n):
            return tiles_ps[n % 2][:, :, 0:HALF]

        def misc_halves(first):
            return misc[:, first:first + 1024].rearrange("p (a b) -> p a b", a=2)[:, :, 0:HALF]

        x_landed = [sem(f"x_landed{k}") for k in range(4)]
        consts = sem("consts")
        settled = sem("settled")
        w_landed = [sem(f"w_landed{k}") for k in range(RING)]
        w_hi_done = sem("w_hi_done")
        w_split = sem("w_split")
        units_begun = sem("units_begun")
        tile_done = sem("tile_done")
        tile_free = [sem(f"tile_free{k}") for k in range(2)]
        masks = sem("masks")
        zeroed_p, zeroed_v = sem("zeroed_p"), sem("zeroed_v")
        ln_cent, ln_sq, ln_s1, ln_s2 = sem("ln_cent"), sem("ln_sq"), sem("ln_s1"), sem("ln_s2")
        ln_mm, ln_sd, ln_rstd = sem("ln_mm"), sem("ln_sd"), sem("ln_rstd")
        ln_var = sem("ln_var")
        ln_sub, ln_mul, ln_h, ln_scaled = sem("ln_sub"), sem("ln_mul"), sem("ln_h"), sem("ln_scaled")
        x_hi_done, x_ready = sem("x_hi_done"), sem("x_ready")
        z_ready, swapped, cos_done, rot_ready = sem("z_ready"), sem("swapped"), sem("cos_done"), sem("rot_ready")
        op_act, op_dve, op_pool = sem("op_act"), sem("op_dve"), sem("op_pool")
        va_ready, va_turned, sv_ready = sem("va_ready"), sem("va_turned"), sem("sv_ready")
        kv_out = sem("kv_out")
        wf_hi_done, wf_split = sem("wf_hi_done"), sem("wf_split")
        f_exp, f_arg, f_log, f_w, f_sum, f_hi, f_rows, f_saved = (sem(n) for n in (
            "f_exp", "f_arg", "f_log", "f_w", "f_sum", "f_hi", "f_rows", "f_saved"))
        clogf_landed = sem("clogf_landed")
        scored = sem("scored")
        negmax = sem("negmax")
        exp_done = sem("exp_done")
        normed = sem("normed")
        turned = sem("turned")
        turn_out = sem("turn_out")
        weighed = sem("weighed")
        out_free = sem("out_free")
        v_ready, v_turned, fv_ready = sem("v_ready"), sem("v_turned"), sem("fv_ready")
        k_ready = sem("k_ready")
        v_out, k_out, forget_rows = sem("v_out"), sem("k_out"), sem("forget_rows")
        ck_landed, cv_landed = sem("ck_landed"), sem("cv_landed")
        relu_done, hsq_done, hid_hi_done, hid_ready = sem("relu_done"), sem("hsq_done"), sem("hid_hi_done"), sem("hid_ready")
        y_sum, y_ready = sem("y_sum"), sem("y_ready")
        p_landed, p_hi_done, p_ready, pe_ready = sem("p_landed"), sem("p_hi_done"), sem("p_ready"), sem("pe_ready")
        gate, gated = sem("gate"), sem("gated")
        y_out = [sem("y_out0"), sem("y_out1")]
        ch_act, ch_dve, ch_pool = sem("ch_act"), sem("ch_dve"), sem("ch_pool")

        OP_KV = 4
        OP_FOX_A = OP_KV + 2 * PAIRS
        OP_FOX_P = OP_KV

        def wait_freed(eng, n, i=None, dn=0):
            k, count = freed(n)
            eng.wait_ge(tile_free[k], lin(count, i, dn // 2))

        def sink_col(pair, head, i, dp):
            if i is None:
                return sinks[:, 2 * pair + head:2 * pair + head + 1]
            return sinks[:, bass.ds(i * (2 * dp) + (2 * pair + head), 1)]

        def settle(eng):
            eng.sem_inc(settled, 1)

        block = outer.enter_context(nc.Block())

        ZERO_SWA, ZERO_ALL = 3, 3 + 8
        f_tmp = acc[0:16, :, :].rearrange("p k t -> p (k t)")

        def f_row(col, n):
            return f_tmp[:, col:col + n]

        @block.sync
        def _(sp):
            for k in range(4):
                sp.dma_start(acc[:, 4 * k:4 * k + 4, :], t["x"][:, 4 * k:4 * k + 4, :]).then_inc(x_landed[k], 16)
            with sp.Fori(0, UNITS // RING) as r:
                for s in range(RING):
                    sp.wait_ge(w_split, r * RING + (s + 1))
                    sp.dma_start(w_raw[:, s, :], t["w"][bass.ds(r * RING + s, 1), :, :].rearrange("o p c -> p (o c)"))\
                        .then_inc(w_landed[s], 16)

        @block.tensor
        def _(pe):
            def products(dst, hi, lo, xh, xl, first, last, begin=False):
                ins = None
                for a, (w, x) in enumerate(((hi, xh), (hi, xl), (lo, xh))):
                    for h in range(2):
                        ins = nc.tensor.matmul(dst[:, h, :], w, x[:, h * HALF:(h + 1) * HALF],
                                               start=first and a == 0, stop=last and a == 2)
                        if begin and a == 0 and h == 0:
                            ins.then_inc(units_begun, 1)
                return ins

            def tile(n, u, i=None, dn=0, du=0, x_gen=None, between=None, c0=0):
                wait_freed(pe, n - 2, i, dn)
                for c in range(KT):
                    if between:
                        between(c0 + c)
                    if c % 8 == 0:
                        pe.wait_ge(w_split, lin(RING + u + c // 8 + 1, i, du))
                    if x_gen is not None:
                        pe.wait_ge(x_ready, 2 + KT * x_gen + c + 1)
                    slot = (u + c // 8) % RING
                    cut = slice(128 * (c % 8), 128 * (c % 8) + 128)
                    ins = products(tile_ps(n), w_hi[:, slot, cut], w_lo[:, slot, cut], x_hi[:, c, :], x_lo[:, c, :],
                                   c == 0, c == KT - 1, begin=c % 8 == 0)
                ins.then_inc(tile_done, 1)

            def down_unit(n, u, hs, i=None, dn=0, du=0, between=None):
                pe.wait_ge(w_split, lin(RING + u + 1, i, du))
                slot = u % RING
                for j in range(2):
                    wait_freed(pe, n + j - 2, i, dn)
                    for k in range(4):
                        cut = slice(256 * k + 128 * j, 256 * k + 128 * j + 128)
                        ins = products(tile_ps(n + j), w_hi[:, slot, cut], w_lo[:, slot, cut], hid_hi[:, hs, k, :],
                                       hid_lo[:, hs, k, :], k == 0, k == 3, begin=j == 0 and k == 0)
                    ins.then_inc(tile_done, 1)

            def ln_shift(src):
                for h in range(2):
                    ins = nc.tensor.matmul(misc_halves(0)[:, h, :], mean_w[:, :], halves(src)[:, h, :], start=True, stop=True)
                ins.then_inc(ln_mm, 1)

            def ln_sums(L):
                pe.wait_ge(ln_s1, 1 + KT * (L + 1))
                pe.wait_ge(ln_s2, 1 + KT * (L + 1))
                for k, s in enumerate((S1, S2)):
                    for h in range(2):
                        ins = nc.tensor.matmul(misc_halves(1024 * k)[:, h, :], mean_w[:, :], halves(s)[:, h, :],
                                               start=True, stop=True)
                ins.then_inc(ln_mm, 1)

            def attend(kind, j, pair, i=None, dp=0):
                g0, dg = STEPS * pair, STEPS * dp
                q1, k1, k2 = (sq1, sk1, sk2) if kind == "swa" else (fq1, fk1, fk2)
                p, pt = (s_p, s_pt) if kind == "swa" else (f_p, f_pt)
                if j < STEPS:
                    head, qt = step_of(j)
                    both = kind == "fox" and qt == 4
                    pe.wait_ge(exp_done, lin(g0 + j + (2 if both else 1), i, dg))
                    lhs = slice(128 * qt, 128 * qt + 128) if qt < 4 else slice(TOK - 128, TOK)
                    ins = None

                    def score(at, width, ka, kb, key, mask=None):
                        dst = scores_ps[:, at:at + width]
                        qb = q1 if kind == "swa" else fq2
                        nc.tensor.matmul(dst, q1[:, head, lhs], ka[:, head, key:key + width], start=True, stop=False)
                        last = nc.tensor.matmul(dst, qb[:, head, lhs], kb[:, head, key:key + width], start=False,
                                                stop=mask is None)
                        if mask is not None:
                            m, mw = mask
                            last = nc.tensor.matmul(scores_ps[:, at + width - mw:at + width], ident_r[:, :], m,
                                                    start=False, stop=True)
                        return last
                    at = 512 * (j % 2)
                    if kind == "swa":
                        if qt == 0:
                            score(at, 128, k1, k2, 0, (win_r[:, 128:256], 128))
                        elif qt < 4:
                            score(at, 256, k1, k2, 128 * (qt - 1), (win_r[:, :], 256))
                        else:
                            score(at, 128, k1, k2, CACHE_COL)
                            score(at + WIN, SAMPLE, k1, k2, PROMPT)
                        end = at + span(kind, j)[1]
                        ins = nc.tensor.matmul(scores_ps[:, end - 1:end], ident[:, :], sink_col(pair, head, i, dp),
                                               start=True, stop=True)
                    else:
                        if qt < 4:
                            ins = score(at, 128 * (qt + 1), k1, k2, 0, (tri_r[:, :], 128))
                        else:
                            score(0, PAST, fc1, fc2, 0)
                            ins = score(512, SAMPLE, k1, k2, PROMPT, (tri_r[:, 64:128], SAMPLE))
                    ins.then_inc(scored, 1)
                if 2 <= j <= STEPS + 1:
                    s = j - 2
                    head, qt = step_of(s)
                    pe.wait_ge(normed, lin(g0 + s + 1, i, dg))
                    pe.wait_ge(turn_out, lin(g0 + s + 1, i, dg))
                    if qt == 4 and i is not None:
                        settle(pe)
                    for k, col in enumerate(key_cols(kind, qt)):
                        if qt < 4:
                            ins = nc.tensor.transpose(turn_ps[:, 128 * k:128 * k + 128], p[:, s % 3, col:col + 128], ident[:, :])
                        else:
                            ins = nc.tensor.transpose(turn_ps[:, 64 * k:64 * k + 64], p[64:128, s % 3, col:col + 128],
                                                      ident[64:128, 64:128])
                    ins.then_inc(turned, 1)
                if j >= 3:
                    s = j - 3
                    head, qt = step_of(s)
                    pe.wait_ge(turn_out, lin(g0 + s + 2, i, dg))
                    if s in (0, 8):
                        pe.wait_ge(out_free, lin(2 * pair + 1 + s // 8, i, 2 * dp))
                    if s == 8 and kind == "fox":
                        pe.wait_ge(cv_landed, lin(16 * (pair - PAIRS) + 16, i, 16 * dp))
                    width = 128 if qt < 4 else SAMPLE
                    dst = out_ps[64 * head:64 * head + 64, 128 * qt:128 * qt + 128] if qt < 4 else \
                        out_ps[64 * head:64 * head + 64, 0:SAMPLE]
                    vals = value_tiles(kind, qt)
                    for k, (vt, at) in enumerate(vals):
                        ins = nc.tensor.matmul(dst, vt[:, at, 64 * head:64 * head + 64],
                                               pt[:, s % 2, width * k:width * k + width],
                                               start=k == 0, stop=k == len(vals) - 1)
                    ins.then_inc(weighed, 1)

            def key_cols(kind, qt):
                if kind == "swa":
                    return [0] if qt == 0 else [0, 128]
                return [128 * k for k in range(qt + 1)]

            def value_tiles(kind, qt):
                if kind == "swa":
                    return [(sv, 0)] if qt == 0 else [(sv, qt - 1), (sv, qt)] if qt < 4 else [(sv, 5), (sv, 4)]
                return [(fv, k) for k in range(qt + 1)] if qt < 4 else [(c_v, k) for k in range(4)] + [(fv, 4)]

            def turn_values(src):
                for k in range(4):
                    nc.tensor.transpose(scores_ps[:, 128 * k:128 * k + 128], src[:, 128 * k:128 * k + 128], ident[:, :])
                return nc.tensor.transpose(scores_ps[0:64, 512:640], src[:, 512:576], ident[:, :])

            pe.wait_ge(x_landed[0], 16)
            pe.wait_ge(zeroed_v, 1)
            ln_shift(acc[:, 0, :])
            pe.wait_ge(consts, 16 * N_CONSTS)
            ln_sums(0)
            tile(0, U_KV, x_gen=0)

            def rotate(r, n, i=None, dr=0):
                pe.wait_ge(z_ready, lin(r + 1, i, dr))
                for h in range(2):
                    ins = nc.tensor.matmul(tile_ps(n)[:, h, :], swap[:, :], z_t[:, h * HALF:(h + 1) * HALF], start=True, stop=True)
                ins.then_inc(swapped, 1)

            tile(1, U_KV + 2, between=lambda c: rotate(0, 0) if c == 4 else None)
            pe.wait_ge(wf_split, 1)
            wait_freed(pe, 0)
            for c in range(KT):
                ins = products(tile_ps(2)[0:16], wf_hi[:, 16 * c:16 * c + 16], wf_lo[:, 16 * c:16 * c + 16],
                               x_hi[:, c, :], x_lo[:, c, :], c == 0, c == KT - 1)
            ins.then_inc(tile_done, 1)
            wait_freed(pe, 1)
            pe.wait_ge(ln_var, 1)
            turn_values(va_t).then_inc(va_turned, 1)

            def swa_between(c, pair, i=None, dp=0):
                if c == 2:
                    rotate(pair + 1, T_QA + pair, i, dp)
                if c == 4:
                    pe.wait_ge(op_dve, lin(OP_KV + 2 * pair + 2, i, 2 * dp))
                for j in SWA_SLOTS.get(c, ()):
                    attend("swa", j, pair, i, dp)

            def swa_keys_ready():
                pe.wait_ge(op_dve, OP_KV)
                pe.wait_ge(op_pool, OP_KV)
                pe.wait_ge(zeroed_p, ZERO_SWA)
                pe.wait_ge(sv_ready, 2)
                pe.wait_ge(masks, 3)
            tile(T_QA, U_QA, between=lambda c: swa_keys_ready() if c == 15 else None)
            with pe.Fori(0, 3) as i:
                for j in range(2):
                    tile(T_QA + 1 + j, U_QA + 2 + 2 * j, i, 2, 4, between=lambda c, j=j: swa_between(c, j, i, 2))
            tile(T_QA + 7, U_QA + 14, between=lambda c: swa_between(c, 6))
            for c in range(KT):
                swa_between(c, 7)

            def fox_between(c, q, i=None, dp=0):
                pair = PAIRS + q
                if c == 2:
                    wait_freed(pe, T_FOX + 3 * q, i, 3 * dp)
                    pe.wait_ge(exp_done, lin(STEPS * pair + 2, i, STEPS * dp))
                    turn_values(v_t).then_inc(v_turned, 1)
                if c == 4:
                    pe.wait_ge(fv_ready, lin(2 * q + 2, i, 2 * dp))
                    pe.wait_ge(op_dve, lin(OP_FOX_A + 6 * q + 6, i, 6 * dp))
                    pe.wait_ge(op_pool, lin(OP_FOX_P + 6 * q + 6, i, 6 * dp))
                    pe.wait_ge(forget_rows, lin(96 * q + 96, i, 96 * dp))
                    pe.wait_ge(zeroed_p, ZERO_ALL)
                for j in FOX_SLOTS.get(c, ()):
                    attend("fox", j, pair, i, dp)

            def fox_tiles(q, att, i=None, dp=0):
                for k in range(3):
                    tile(T_FOX + 3 * q + k, U_FOX + 6 * q + 2 * k, i, 3 * dp, 6 * dp,
                         between=None if att is None else (lambda c: fox_between(c, att, i, dp)), c0=KT * k)

            fox_tiles(0, None)
            with pe.Fori(0, 3) as i:
                for j in range(2):
                    fox_tiles(1 + j, j, i, 2)
            fox_tiles(7, 6)
            for c in range(3 * KT):
                fox_between(c, 7)

            tile(T_O, U_O, x_gen=1)

            def first_shift(c):
                if c == 6:
                    wait_freed(pe, T_O)
                    ln_shift(y[:, 0, :])
            tile(T_O + 1, U_O + 2, between=first_shift)
            with pe.Fori(0, 7) as i:
                for j in range(2):
                    tile(T_O + 2 + j, U_O + 4 + 2 * j, i, 2, 4)
            ln_sums(1)

            def up(n, u, i=None, dn=0, du=0, x_gen=None):
                for k in range(4):
                    tile(n + k, u + 2 * k, i, dn, du, x_gen=x_gen if k == 0 else None)

            def down(n, u, fb, i=None, dn=0, du=0, df=0):
                pe.wait_ge(hid_ready, lin(4 * fb + 4, i, 4 * df))
                for k in range(8):
                    down_unit(n + 2 * k, u + k, fb % 2, i, dn, du)

            up(T_MLP, U_MLP, x_gen=2)
            with pe.Fori(0, 7) as i:
                for j in range(2):
                    up(T_MLP + 4 + 20 * j, U_MLP + 8 + 16 * j, i, 40, 32)
                    down(T_MLP + 8 + 20 * j, U_MLP + 16 + 16 * j, j, i, 40, 32, 2)
            up(T_MLP + 284, U_MLP + 232)
            down(T_MLP + 288, U_MLP + 240, 14)
            pe.wait_ge(hid_ready, 64)
            for k in range(8):
                if k == 1:
                    wait_freed(pe, T_MLP + 304)
                    ln_shift(acc[:, 0, :])
                down_unit(T_MLP + 304 + 2 * k, U_MLP + 248 + k, 1)

            pe.wait_ge(p_ready, 1)
            for u in range(4):
                pe.wait_ge(w_split, RING + U_PE + u + 1)
                for j in range(4):
                    n = T_PE + 4 * u + j
                    wait_freed(pe, n - 2)
                    for k in range(2):
                        cut = slice(512 * k + 128 * j, 512 * k + 128 * j + 128)
                        ins = products(tile_ps(n), w_hi[:, u, cut], w_lo[:, u, cut], p_hi[:, k, :], p_lo[:, k, :],
                                       k == 0, k == 1, begin=j == 0 and k == 0)
                    ins.then_inc(tile_done, 1)
                if u == 1:
                    ln_sums(2)
            tile(T_PG, U_PG, x_gen=3)
            tile(T_PG + 1, U_PG + 2)
            with pe.Fori(0, 7) as i:
                for j in range(2):
                    tile(T_PG + 2 + j, U_PG + 4 + 2 * j, i, 2, 4)

        @block.scalar
        def _(act):
            def copy(out, in_, scale=1.0, func=ACT.Copy):
                return nc.scalar.activation(out, in_, func, scale=scale)

            def split(u, i, du):
                act.wait_ge(w_landed[u % RING], lin(16 * (u // RING) + 16, i, 4 * du))
                act.wait_ge(units_begun, lin(u + 1, i, du))
                copy(w_hi[:, u % RING, :], w_raw[:, u % RING, :]).then_inc(w_hi_done, 1)
            ahead = Ahead(split)

            def ln_square(L, c, src):
                act.wait_ge(ln_cent, c + KT * L + 1)
                act.wait_ge(ln_s2, c + KT * L + 1)
                nc.scalar.activation(WK, src, ACT.Square).then_inc(ln_sq, 1)

            def ln_root(L):
                act.wait_ge(ln_var, L + 1)
                nc.scalar.activation(WK, VAR, ACT.Sqrt).then_inc(ln_sd, 1)

            def ln_apply(L, gen, src, scaled):
                act.wait_ge(ln_rstd, L + 1)
                with act.Fori(0, 8) as i:
                    for j in range(2):
                        kt = i * 2 + j
                        work = st[:, 3 + j, :]
                        act.wait_ge(ln_mul, i * 2 + (KT * L + j + 1))
                        act.wait_ge(x_ready, i * 2 + (KT * gen + j - 2 + 3))
                        if scaled:
                            act.wait_ge(ln_scaled, i * 2 + (j + 1))
                        nc.scalar.activation(work, feature_tile(src, kt), ACT.Identity,
                                             bias=cols[:, bass.ds(kt + (2 * L + 1) * KT, 1)],
                                             scale=cols[:, bass.ds(kt + 2 * L * KT, 1)]).then_inc(ln_h, 1)
                        act.wait_ge(ln_h, i * 2 + (KT * L + j + 1))
                        copy(feature_tile(x_hi, kt), work).then_inc(x_hi_done, 1)

            def attend(kind, j, pair, i=None, dp=0):
                g0, dg = STEPS * pair, STEPS * dp
                p, pt = (s_p, s_pt) if kind == "swa" else (f_p, f_pt)
                if j < STEPS:
                    head, qt = step_of(j)
                    act.wait_ge(negmax, lin(g0 + j + 1, i, dg))
                    act.wait_ge(turned, lin(g0 + 2 + max(0, j - 2), i, dg))
                    at, width = span(kind, j)
                    s = j % 3
                    nc.scalar.activation(p[:, s, 0:width], scores_ps[:, at:at + width], ACT.Exp,
                                         bias=stat[:, s, 0:1], scale=1.0, accum_out=stat[:, s, 1:2]).then_inc(exp_done, 1)
                if 2 <= j <= STEPS + 1:
                    s = j - 2
                    head, qt = step_of(s)
                    act.wait_ge(turned, lin(g0 + s + 3, i, dg))
                    act.wait_ge(weighed, lin(g0 + s + 1, i, dg))
                    width = turn_width(kind, qt)
                    copy(pt[:, s % 2, 0:width], turn_ps[:, 0:width]).then_inc(turn_out, 1)
                if j in (11, 13):
                    act.wait_ge(weighed, lin(g0 + 2 + (8 if j == 11 else 10), i, dg))
                    kt = lin(pair, i, dp)
                    dst = feature_tile(acc, kt)
                    if j == 11:
                        copy(dst[:, 0:PROMPT], out_ps[:, :]).then_inc(out_free, 1)
                    else:
                        copy(dst[:, PROMPT:TOK], out_ps[:, 0:SAMPLE]).then_inc(out_free, 1)

            act.sem_inc(exp_done, 2)
            act.sem_inc(turn_out, 1)
            act.sem_inc(out_free, 1)
            for dst, name in ((ident, "ident"), (cols, "cols"), (cos_t, "cos"), (sin_t, "sin"), (swap, "swap"), (win_f, "win"),
                              (tri_f, "tri"), (sinks, "sinks"), (wf, "wf"), (bf, "bf"), (ck_t, "swa_ck"), (cv_t, "swa_cv_t")):
                act.dma_start(dst[:, :], t[name]).then_inc(consts, 16)
            act.dma_start(sv[:, 5, :], t["swa_cv"]).then_inc(consts, 16)
            act.wait_ge(consts, 16 * N_CONSTS)
            copy(ident_r[:, :], ident[:, :]).then_inc(masks, 1)
            copy(tri_r[:, :], tri_f[:, :]).then_inc(masks, 1)
            copy(win_r[:, :], win_f[:, :]).then_inc(masks, 1)
            copy(wf_hi[:, :], wf[:, :]).then_inc(wf_hi_done, 1)
            for c in range(KT):
                ln_square(0, c, acc[:, c, :])
            ln_root(0)
            ahead.upto(1)
            ln_apply(0, 0, acc, False)

            def window(dst, src, n):
                copy(dst[0:64, 0, n[0]:n[1]], src[0:64, :], SCALE if dst is sq1 else 1.0).then_inc(op_act, 1)
                copy(dst[64:128, 1, n[0]:n[1]], src[64:128, :], SCALE if dst is sq1 else 1.0).then_inc(op_act, 1)

            window(sk1, ck_t, (CACHE_COL, CACHE_COL + WIN))
            ahead.upto(3)
            act.wait_ge(tile_done, 1)
            copy(halves(z_t[:, :]), tile_ps(0)).then_inc(z_ready, 1)
            ahead.upto(5)
            act.wait_ge(rot_ready, 1)
            window(sk1, rot, (0, TOK))
            act.wait_ge(tile_done, 2)
            copy(halves(va_t[:, :]), tile_ps(1)).then_inc(tile_free[1], 1)
            act.wait_ge(f_arg, 1)
            nc.scalar.activation(f_tmp[:, F_E:F_E + TOK], f_tmp[:, F_X:F_X + TOK], ACT.Exp, scale=-1.0).then_inc(f_exp, 1)
            act.wait_ge(f_w, 1)
            nc.scalar.activation(f_tmp[:, F_L:F_L + TOK], f_tmp[:, F_W:F_W + TOK], ACT.Ln).then_inc(f_log, 1)
            act.wait_ge(f_sum, 1)
            copy(f_tmp.bitcast(f32r)[:, F_HI:F_HI + TOK + PAST], f_tmp[:, F_SUM:F_SUM + TOK + PAST]).then_inc(f_hi, 1)
            act.wait_ge(va_turned, 1)
            copy(sv[:, 0:4, :], scores_ps[:, 0:512].rearrange("p (a b) -> p a b", a=4)).then_inc(sv_ready, 1)
            copy(sv[0:64, 4, :], scores_ps[0:64, 512:640]).then_inc(sv_ready, 1)

            def swa_pair(q, att, i=None, dp=0):
                for c in range(KT + 1):
                    if c % 8 == 0 and c < KT and q is not None:
                        ahead.upto(U_QA + 2 * q + c // 8 + 2, i, 2 * dp)
                    if att is None:
                        continue
                    if c == 1:
                        act.wait_ge(tile_done, lin(T_QA + att + 1, i, dp))
                        act.wait_ge(swapped, lin(att + 1, i, dp))
                        act.wait_ge(cos_done, lin(att + 1, i, dp))
                        copy(halves(z_t[:, :]), tile_ps(T_QA + att)).then_inc(z_ready, 1)
                    if c == 2:
                        act.wait_ge(rot_ready, lin(att + 2, i, dp))
                        window(sq1, rot, (0, TOK))
                    for j in SWA_SLOTS.get(c, ()) if c < KT else (SLOTS,):
                        attend("swa", j, att, i, dp)

            swa_pair(0, None)
            act.wait_ge(f_saved, 16 * 13)
            with act.Fori(0, 3) as i:
                for j in range(2):
                    swa_pair(1 + j, j, i, 2)
            ahead.leave(3, 4)
            swa_pair(7, 6)
            swa_pair(None, 7)

            def own(dst, src, n, scale=1.0):
                copy(dst[0:64, 0, 0:n], src[0], scale).then_inc(op_act, 1)
                copy(dst[64:128, 1, 0:n], src[1], scale).then_inc(op_act, 1)

            def fox_pair(q, att, i=None, dp=0):
                for c in range(3 * KT):
                    if c % 8 == 0 and q is not None:
                        ahead.upto(U_FOX + 6 * q + c // 8 + 2, i, 6 * dp)
                    if att is not None:
                        if c == 0:
                            act.wait_ge(tile_done, lin(T_FOX + 3 * att + 3, i, 3 * dp))
                            ps = tile_ps(T_FOX + 3 * att + 2)
                            copy(halves(fq1[0:64, 0, :]), ps[0:64], SCALE).then_inc(op_act, 1)
                            copy(halves(fq1[64:128, 1, :]), ps[64:128], SCALE).then_inc(op_act, 1)
                        if c == 2:
                            act.wait_ge(v_turned, lin(att + 1, i, dp))
                            copy(fv[:, 0:4, :], scores_ps[:, 0:512].rearrange("p (a b) -> p a b", a=4)).then_inc(fv_ready, 1)
                            copy(fv[0:64, 4, :], scores_ps[0:64, 512:640]).then_inc(fv_ready, 1)
                        for j in FOX_SLOTS.get(c, ()) if c != 42 else (SLOTS,):
                            attend("fox", j, PAIRS + att, i, dp)
                    if q is not None:
                        if c == 17:
                            act.wait_ge(tile_done, lin(T_FOX + 3 * q + 1, i, 3 * dp))
                            if q:
                                act.wait_ge(v_out, lin(16 * q, i, 16 * dp))
                            copy(halves(v_t[:, :]), tile_ps(T_FOX + 3 * q)).then_inc(tile_free[(T_FOX + 3 * q) % 2], 1)
                        if c == 33:
                            act.wait_ge(tile_done, lin(T_FOX + 3 * q + 2, i, 3 * dp))
                            if q:
                                act.wait_ge(k_out, lin(16 * q, i, 16 * dp))
                            copy(halves(k_t[:, :]), tile_ps(T_FOX + 3 * q + 1))\
                                .then_inc(tile_free[(T_FOX + 3 * q + 1) % 2], 1)
                            wait_freed(act, T_FOX + 3 * q + 1, i, 3 * dp)
                            own(fk1, (k_t[0:64, :], k_t[64:128, :]), TOK)
                        if c == 34:
                            act.wait_ge(ck_landed, lin(16 * q + 16, i, 16 * dp))
                            own(fc1, (c_t[0:64, :], c_t[64:128, :]), PAST)

            fox_pair(0, None)
            with act.Fori(0, 3) as i:
                for j in range(2):
                    fox_pair(1 + j, j, i, 2)
            ahead.leave(3, 12)
            fox_pair(7, 6)
            fox_pair(None, 7)

            for c in range(KT):
                act.wait_ge(y_sum, c + 1)
                if c == 0:
                    act.wait_ge(out_free, 1 + 4 * PAIRS)
                copy(x_hi[:, c, :], acc[:, c, :]).then_inc(x_hi_done, 1)
            ahead.upto(U_O + 3)
            ahead.upto(U_O + 5)
            ln_square(1, 0, y[:, 0, :])
            with act.Fori(0, 7) as i:
                for j in range(2):
                    ahead.upto(U_O + 4 + 2 * j + 3, i, 4)
                    act.wait_ge(ln_cent, i * 2 + (KT + j + 2))
                    act.wait_ge(ln_s2, i * 2 + (KT + j + 2))
                    nc.scalar.activation(WK, feature_tile(y, i * 2 + (j + 1)), ACT.Square).then_inc(ln_sq, 1)
            ahead.leave(7, 4)
            ln_square(1, 15, y[:, 15, :])
            ln_root(1)
            ln_apply(1, 2, y, True)

            def hidden(n, m, i=None, dn=0, dm=0):
                act.wait_ge(tile_done, lin(n + 1, i, dn))
                act.wait_ge(hsq_done, lin(m + 1, i, dm))
                nc.scalar.activation(halves(WK), tile_ps(n), ACT.Relu).then_inc(tile_free[n % 2], 1)

            def hidden_hi(m, i=None, dm=0):
                act.wait_ge(hsq_done, lin(m + 2, i, dm))
                copy(hid_hi[:, m // 4 % 2, m % 4, :], WK2).then_inc(hid_hi_done, 1)

            def up(n, u, m, i=None, dn=0, du=0, dm=0):
                for k in range(4):
                    ahead.upto(u + 2 * k + 3, i, du)
                    hidden(n + k, m + k, i, dn, dm)
                    hidden_hi(m + k, i, dm)

            def down(u, i=None, du=0):
                for k in range(8):
                    ahead.upto(u + k + 2, i, du)

            act.wait_ge(ln_scaled, 2 + KT)
            act.wait_ge(x_ready, 2 + 3 * KT)
            up(T_MLP, U_MLP, 0)
            act.wait_ge(p_landed, 16)
            copy(p_hi[:, :, :], p_raw[:, :, :]).then_inc(p_hi_done, 1)
            with act.Fori(0, 7) as i:
                for j in range(2):
                    up(T_MLP + 4 + 20 * j, U_MLP + 8 + 16 * j, 4 + 4 * j, i, 40, 32, 8)
                    down(U_MLP + 16 + 16 * j, i, 32)
            ahead.leave(7, 32)
            up(T_MLP + 284, U_MLP + 232, 60)
            down(U_MLP + 240)
            for n in range(KT):
                ahead.upto(U_MLP + 248 + n // 2 + 2)
                if n >= 1:
                    ln_square(2, n - 1, acc[:, n - 1, :])
            ln_square(2, 15, acc[:, 15, :])

            for n in range(T_PE, T_PE + KT):
                ahead.upto(U_PE + (n - T_PE) // 4 + 2)
                act.wait_ge(tile_done, n + 1)
                copy(halves(pe_out[:, n - T_PE, :]), tile_ps(n)).then_inc(tile_free[n % 2], 1)
                if n == T_PE + 8:
                    ln_root(2)
            ln_apply(2, 3, acc, False)

            def gate_tile(n, u, i=None, dn=0, du=0):
                kt = lin(n - T_PG, i, dn)
                ahead.upto(u + 3, i, du)
                act.wait_ge(tile_done, lin(n + 1, i, dn))
                act.wait_ge(gated, lin(n - T_PG + 1, i, dn))
                bias = cols[:, 6 * KT + kt:6 * KT + kt + 1] if i is None else cols[:, bass.ds(kt + 6 * KT, 1)]
                nc.scalar.activation(halves(st[:, n % 2, :]), tile_ps(n), ACT.Sigmoid, bias=bias)\
                    .then_inc(tile_free[n % 2], 1)

            for j in range(2):
                gate_tile(T_PG + j, U_PG + 2 * j)
            with act.Fori(0, 6) as i:
                for j in range(2):
                    gate_tile(T_PG + 2 + j, U_PG + 4 + 2 * j, i, 2, 4)
            ahead.leave(6, 4)
            for j in range(14, 16):
                gate_tile(T_PG + j, U_PG + 2 * j)

        @block.vector
        def _(dve):
            chain = Chain(dve, ch_dve)
            V = nc.vector

            def split(u, i, du):
                dve.wait_ge(w_hi_done, lin(u + 1, i, du))
                V.tensor_tensor(w_lo[:, u % RING, :], w_raw[:, u % RING, :], w_hi[:, u % RING, :], ALU.subtract)\
                    .then_inc(w_split, 1)
            ahead = Ahead(split)

            def ln_take_shift(L):
                dve.wait_ge(ln_mm, 2 * L + 1)
                chain.add(V.tensor_scalar(halves(SH), misc_halves(0), float(KT), None, ALU.mult))
                chain.wait()

            def ln_center(tile):
                V.tensor_tensor(tile, tile, SH, ALU.subtract).then_inc(ln_cent, 1)

            def ln_add(c, i=None):
                dve.wait_ge(ln_sq, lin(c + 1, i, 2))
                dve.wait_ge(ln_s2, lin(c + 1, i, 2))
                V.tensor_tensor(S2, S2, WK, ALU.add).then_inc(ln_s2, 1)

            def ln_finish(L):
                dve.wait_ge(ln_mm, 2 * L + 2)
                chain.add(V.tensor_copy(halves(MU), misc_halves(0)))
                chain.wait()
                chain.add(V.scalar_tensor_tensor(VAR, MU, -1.0, MU, ALU.mult, ALU.mult))
                chain.wait()
                V.scalar_tensor_tensor(halves(VAR), halves(VAR), EPS, misc_halves(1024), ALU.add, ALU.add).then_inc(ln_var, 1)
                dve.wait_ge(ln_sd, L + 1)
                chain.add(V.reciprocal(RSTD, WK))
                chain.wait()
                chain.add(V.scalar_tensor_tensor(WK2, RSTD, -0.5, RSTD, ALU.mult, ALU.mult))
                chain.wait()
                chain.add(V.tensor_tensor(WK2, WK2, VAR, ALU.mult))
                chain.wait()
                V.scalar_tensor_tensor(RSTD, WK2, 1.5, RSTD, ALU.add, ALU.mult).then_inc(ln_rstd, 1)

            def ln_apply(L, gen, src):
                dve.wait_ge(ln_rstd, L + 1)

                def low(kt, i, c):
                    dve.wait_ge(x_hi_done, lin(KT * gen + c + 1, i, 2))
                    V.tensor_tensor(feature_tile(x_lo, kt), st[:, 3 + c % 2, :], feature_tile(x_hi, kt), ALU.subtract)\
                        .then_inc(x_ready, 1)

                def times(kt, i, c):
                    dve.wait_ge(ln_sub, lin(KT * L + c + 1, i, 2))
                    s = feature_tile(src, kt)
                    V.tensor_tensor(s, s, RSTD, ALU.mult).then_inc(ln_mul, 1)
                times(0, None, 0)
                times(1, None, 1)
                low(0, None, 0)
                with dve.Fori(0, 7) as i:
                    for j in range(2):
                        times(i * 2 + (2 + j), i, 2 + j)
                        low(i * 2 + (1 + j), i, 1 + j)
                low(15, None, 15)

            def attend(kind, j, pair, i=None, dp=0):
                g0, dg = STEPS * pair, STEPS * dp
                p = s_p if kind == "swa" else f_p
                if j < STEPS:
                    dve.wait_ge(scored, lin(g0 + j + 1, i, dg))
                    at, width = span(kind, j)
                    V.reduce_max(stat[:, j % 3, 0:1], scores_ps[:, at:at + width], AX, negate=True).then_inc(negmax, 1)
                if 1 <= j <= STEPS:
                    s = (j - 1) % 3
                    dve.wait_ge(exp_done, lin(g0 + j + 2, i, dg))
                    at, width = span(kind, j - 1)
                    chain.add(V.reciprocal(stat[:, s, 2:3], stat[:, s, 1:2]))
                    chain.wait()
                    V.tensor_scalar(p[:, s, 0:width], p[:, s, 0:width], stat[:, s, 2:3], None, ALU.mult)\
                        .then_inc(normed, 1)

            dve.sem_inc(w_split, RING)
            dve.sem_inc(tile_free[0], 1)
            dve.sem_inc(tile_free[1], 1)
            dve.sem_inc(hsq_done, 1)
            dve.sem_inc(x_ready, 2)
            dve.sem_inc(gated, 2)
            chain.add(V.memset(S2, 0.0))
            V.memset(mean_w[:, :], 1.0 / D).then_inc(zeroed_v, 1)
            chain.wait()
            dve.sem_inc(ln_s2, 1)
            dve.wait_ge(x_landed[0], 16)
            ln_take_shift(0)
            for c in range(KT):
                if c % 4 == 0:
                    dve.wait_ge(x_landed[c // 4], 16)
                ln_center(acc[:, c, :])
                if c >= 1:
                    ln_add(c - 1)
            ln_add(15)
            dve.wait_ge(wf_hi_done, 1)
            V.tensor_tensor(wf_lo[:, :], wf[:, :], wf_hi[:, :], ALU.subtract).then_inc(wf_split, 1)
            ln_finish(0)
            ahead.upto(1)
            ln_apply(0, 0, acc)

            def lows(pairs, count, i=None, dc=0):
                for (dst, src, hi, scale), k in zip(pairs, range(len(pairs))):
                    dve.wait_ge(op_act, lin(count + k + 1, i, dc))
                    ins = V.scalar_tensor_tensor(dst, src, scale, hi, ALU.mult, ALU.subtract).then_inc(op_dve, 1)
                return ins

            cc = slice(CACHE_COL, CACHE_COL + WIN)
            lows([(sk2[0:64, 0, cc], ck_t[0:64, :], sk1[0:64, 0, cc], 1.0),
                  (sk2[64:128, 1, cc], ck_t[64:128, :], sk1[64:128, 1, cc], 1.0)], 0)
            ahead.upto(3)

            def rotate(r, n, i=None, dr=0):
                dve.wait_ge(swapped, lin(r + 1, i, dr))
                V.tensor_tensor(halves(rot2[:, :]), tile_ps(n), halves(sin_t[:, :]), ALU.mult).then_inc(tile_free[n % 2], 1)
                dve.wait_ge(cos_done, lin(r + 1, i, dr))
                wait_freed(dve, n, i, dr)
                V.tensor_tensor(rot[:, :], rot[:, :], rot2[:, :], ALU.add).then_inc(rot_ready, 1)
                dve.wait_ge(rot_ready, lin(r + 1, i, dr))

            rotate(0, 0)
            lows([(sk2[0:64, 0, 0:TOK], rot[0:64, :], sk1[0:64, 0, 0:TOK], 1.0),
                  (sk2[64:128, 1, 0:TOK], rot[64:128, :], sk1[64:128, 1, 0:TOK], 1.0)], 2)
            ahead.upto(5)

            def row(col, n=TOK):
                return f_tmp[:, col:col + n]
            dve.wait_ge(tile_done, 3)
            dve.wait_ge(ln_h, KT)
            V.tensor_scalar(halves(row(F_D)), tile_ps(2)[0:16], bf[:, :], None, ALU.add).then_inc(tile_free[0], 1)
            wait_freed(dve, 2)
            V.scalar_tensor_tensor(row(F_X), row(F_D), -1.0, row(F_D), ALU.mult, ALU.max).then_inc(f_arg, 1)
            chain.add(V.tensor_scalar(row(F_M), row(F_D), 0.0, None, ALU.min))
            dve.wait_ge(f_exp, 1)
            V.tensor_scalar(row(F_W), row(F_E), 1.0, None, ALU.add).then_inc(f_w, 1)
            dve.wait_ge(f_w, 1)
            chain.wait()
            chain.add(V.tensor_scalar(row(F_D), row(F_W), -1.0, None, ALU.add))
            chain.wait()
            chain.add(V.tensor_scalar(row(F_R), row(F_D), 2.0 ** -23, None, ALU.max))
            chain.wait()
            chain.add(V.reciprocal(row(F_R), row(F_R)))
            chain.wait()
            chain.add(V.tensor_tensor(row(F_R), row(F_R), row(F_E), ALU.mult))
            chain.wait()
            dve.wait_ge(f_log, 1)
            chain.add(V.tensor_tensor(row(F_L), row(F_L), row(F_R), ALU.mult))
            chain.add(V.scalar_tensor_tensor(row(F_D), row(F_D), 0.0, row(F_E), ALU.is_equal, ALU.mult))
            chain.wait()
            chain.add(V.tensor_tensor(row(F_L), row(F_L), row(F_D), ALU.add))
            chain.wait()
            chain.add(V.tensor_tensor(row(F_G), row(F_M), row(F_L), ALU.subtract))
            chain.add(V.memset(row(F_X), 0.0))
            chain.wait()
            dve.wait_ge(clogf_landed, 16)
            chain.add(V.tensor_tensor_scan(row(F_SUM, PROMPT), row(F_X, PROMPT), row(F_G, PROMPT), 0.0, ALU.add, ALU.add))
            chain.add(V.tensor_tensor_scan(row(F_SUM + TOK, PAST), row(F_X, PAST), row(F_C, PAST), 0.0, ALU.add, ALU.add))
            chain.wait()
            last = F_SUM + TOK + PAST - 1
            V.tensor_tensor_scan(row(F_SUM + PROMPT, SAMPLE), row(F_X, SAMPLE), row(F_G + PROMPT, SAMPLE),
                                 row(last, 1), ALU.add, ALU.add).then_inc(f_sum, 1)
            dve.wait_ge(f_hi, 1)

            def rounded(col):
                return f_tmp.bitcast(f32r)[:, col:col + F_ALL]
            V.tensor_tensor(rounded(F_LO), row(F_SUM, F_ALL), row(F_HI, F_ALL), ALU.subtract).then_inc(f_rows, 1)
            V.tensor_scalar(rounded(F_NHI), row(F_HI, F_ALL), -1.0, None, ALU.mult).then_inc(f_rows, 1)
            dve.wait_ge(f_rows, 2)
            V.tensor_scalar(rounded(F_NLO), row(F_LO, F_ALL), -1.0, None, ALU.mult).then_inc(f_rows, 1)
            V.memset(row(F_ONE), 1.0).then_inc(f_rows, 1)

            def swa_pair(q, att, i=None, dp=0):
                for c in range(KT):
                    if c % 8 == 0 and q is not None:
                        ahead.upto(U_QA + 2 * q + c // 8 + 2, i, 2 * dp)
                    if att is None:
                        continue
                    if c == 2:
                        rotate(att + 1, T_QA + att, i, dp)
                        lows([(sq1[64:128, 0, :], rot[0:64, :], sq1[0:64, 0, :], SCALE),
                              (sq1[0:64, 1, :], rot[64:128, :], sq1[64:128, 1, :], SCALE)], OP_KV + 2 * att, i, 2 * dp)
                    for j in SWA_SLOTS.get(c, ()):
                        attend("swa", j, att, i, dp)

            swa_pair(0, None)
            with dve.Fori(0, 3) as i:
                chain.enter(i, 2 * STEPS)
                for j in range(2):
                    swa_pair(1 + j, j, i, 2)
                chain.leave(3)
            ahead.leave(3, 4)
            swa_pair(7, 6)
            swa_pair(None, 7)

            def fox_pair(q, att, i=None, dp=0):
                n0, dn, df = T_FOX + 3 * (q or 0), 3 * dp, 6 * dp
                for c in range(3 * KT):
                    if c % 8 == 0 and q is not None:
                        ahead.upto(U_FOX + 6 * q + c // 8 + 2, i, 6 * dp)
                    if att is not None:
                        if c == 0:
                            n = T_FOX + 3 * att + 2
                            ps = tile_ps(n)
                            lows([(halves(fq1[64:128, 0, :]), ps[0:64], halves(fq1[0:64, 0, :]), SCALE),
                                  (halves(fq1[0:64, 1, :]), ps[64:128], halves(fq1[64:128, 1, :]), SCALE)],
                                 OP_FOX_A + 6 * att + 4, i, df)
                            dve.wait_ge(op_dve, lin(OP_FOX_A + 6 * att + 6, i, df))
                            dve.sem_inc(tile_free[n % 2], 1)
                        for j in FOX_SLOTS.get(c, ()):
                            attend("fox", j, PAIRS + att, i, dp)
                    if q is not None:
                        if c == 33:
                            wait_freed(dve, n0 + 1, i, dn)
                            lows([(fk2[0:64, 0, :], k_t[0:64, :], fk1[0:64, 0, :], 1.0),
                                  (fk2[64:128, 1, :], k_t[64:128, :], fk1[64:128, 1, :], 1.0)], OP_FOX_A + 6 * q, i, df)
                        if c == 34:
                            lows([(fc2[0:64, 0, :], c_t[0:64, :], fc1[0:64, 0, :], 1.0),
                                  (fc2[64:128, 1, :], c_t[64:128, :], fc1[64:128, 1, :], 1.0)], OP_FOX_A + 6 * q + 2, i, df)

            fox_pair(0, None)
            with dve.Fori(0, 3) as i:
                chain.enter(i, 2 * STEPS)
                for j in range(2):
                    fox_pair(1 + j, j, i, 2)
                chain.leave(3)
            ahead.leave(3, 12)
            fox_pair(7, 6)
            fox_pair(None, 7)

            dve.wait_ge(tile_done, T_O)
            dve.wait_ge(out_free, 1 + 4 * PAIRS)
            for c in range(KT):
                V.tensor_tensor(y[:, c, :], x_hi[:, c, :], x_lo[:, c, :], ALU.add).then_inc(y_sum, 1)
                if c == 0:
                    chain.add(V.memset(S2, 0.0))
                dve.wait_ge(x_hi_done, KT + c + 1)
                V.tensor_tensor(x_lo[:, c, :], acc[:, c, :], x_hi[:, c, :], ALU.subtract).then_inc(x_ready, 1)

            def residual(dst, n, i=None, dn=0):
                dve.wait_ge(tile_done, lin(n + 1, i, dn))
                d = feature_tile(dst, lin(n - T_O, i, dn)) if dst is y else dst
                V.tensor_tensor(halves(d), halves(d), tile_ps(n), ALU.add).then_inc(tile_free[n % 2], 1)

            for n in range(T_O, T_O + 2):
                ahead.upto(U_O + 2 * (n - T_O) + 3)
                dve.wait_ge(y_ready, n - T_O + 1)
                residual(y, n)
            ln_take_shift(1)
            wait_freed(dve, T_O)
            ln_center(y[:, 0, :])
            with dve.Fori(0, 7) as i:
                for j in range(2):
                    ahead.upto(U_O + 4 + 2 * j + 3, i, 4)
                    dve.wait_ge(y_ready, i * 2 + (j + 3))
                    residual(y, T_O + 2 + j, i, 2)
                    wait_freed(dve, T_O + 1 + j, i, 2)
                    ln_center(feature_tile(y, i * 2 + (j + 1)))
                    ln_add(KT + j, i)
            ahead.leave(7, 4)
            wait_freed(dve, T_O + 15)
            ln_center(y[:, 15, :])
            ln_add(KT + 14)
            ln_add(KT + 15)
            ln_finish(1)
            ln_apply(1, 2, y)

            def hidden(n, m, i=None, dn=0, dm=0):
                wait_freed(dve, n, i, dn)
                dve.wait_ge(hid_ready, lin(m, i, dm)) if m or i is not None else None
                V.tensor_tensor(WK2, WK, WK, ALU.mult).then_inc(hsq_done, 1)
                dve.wait_ge(hid_hi_done, lin(m + 1, i, dm))
                V.tensor_tensor(hid_lo[:, m // 4 % 2, m % 4, :], WK2, hid_hi[:, m // 4 % 2, m % 4, :], ALU.subtract)\
                    .then_inc(hid_ready, 1)

            def up(n, u, m, i=None, dn=0, du=0, dm=0):
                for k in range(4):
                    ahead.upto(u + 2 * k + 3, i, du)
                    hidden(n + k, m + k, i, dn, dm)

            def down(n, u, i=None, dn=0, du=0):
                for k in range(KT):
                    ahead.upto(u + k // 2 + 2, i, du)
                    residual(acc[:, k, :], n + k, i, dn)

            dve.wait_ge(ln_scaled, 2 + KT)
            up(T_MLP, U_MLP, 0)
            dve.wait_ge(p_hi_done, 1)
            V.tensor_tensor(p_lo[:, :, :], p_raw[:, :, :], p_hi[:, :, :], ALU.subtract).then_inc(p_ready, 1)
            dve.wait_ge(ln_scaled, 2 + KT)
            with dve.Fori(0, 7) as i:
                for j in range(2):
                    up(T_MLP + 4 + 20 * j, U_MLP + 8 + 16 * j, 4 + 4 * j, i, 40, 32, 8)
                    down(T_MLP + 8 + 20 * j, U_MLP + 16 + 16 * j, i, 40, 32)
            ahead.leave(7, 32)
            up(T_MLP + 284, U_MLP + 232, 60)
            down(T_MLP + 288, U_MLP + 240)
            chain.add(V.memset(S2, 0.0))
            for c in range(KT):
                n = T_MLP + 304 + c
                ahead.upto(U_MLP + 248 + c // 2 + 2)
                residual(acc[:, c, :], n)
                if c == 1:
                    ln_take_shift(2)
                if c >= 1:
                    wait_freed(dve, n - 1)
                    ln_center(acc[:, c - 1, :])
                if c >= 2:
                    ln_add(2 * KT + c - 2)
            wait_freed(dve, T_MLP + 319)
            ln_center(acc[:, 15, :])
            ln_add(2 * KT + 14)
            ln_add(2 * KT + 15)
            for u in range(U_PE, U_PE + 4):
                ahead.upto(u + 2)
                if u == U_PE + 1:
                    ln_finish(2)
            ln_apply(2, 3, acc)

            def gate_tile(n, u, i=None, dn=0, du=0):
                kt = lin(n - T_PG, i, dn)
                d = st[:, 2 + n % 2, :]
                ahead.upto(u + 3, i, du)
                wait_freed(dve, n, i, dn)
                if i is not None or n >= T_PG + 2:
                    dve.wait_ge(y_out[n % 2], lin(16 * ((n - T_PG) // 2), i, 16))
                chain.add(V.tensor_tensor(d, st[:, n % 2, :], feature_tile(pe_out, kt), ALU.mult))
                chain.wait()
                chain.add(V.tensor_tensor(d, d, feature_tile(x_hi, kt), ALU.add))
                chain.wait()
                V.tensor_tensor(d, d, feature_tile(x_lo, kt), ALU.add).then_inc(gated, 1)

            for j in range(2):
                gate_tile(T_PG + j, U_PG + 2 * j)
            with dve.Fori(0, 6) as i:
                chain.enter(i, 4)
                for j in range(2):
                    gate_tile(T_PG + 2 + j, U_PG + 4 + 2 * j, i, 2, 4)
                chain.leave(6)
            ahead.leave(6, 4)
            for j in range(14, 16):
                gate_tile(T_PG + j, U_PG + 2 * j)

        @block.gpsimd
        def _(pool):
            P = nc.gpsimd

            def ln_sum(L, src):
                P.memset(S1, 0.0).then_inc(ch_pool, 1)
                pool.wait_ge(ch_pool, L + 1)
                with pool.Fori(0, KT) as i:
                    pool.wait_ge(ln_cent, i + (KT * L + 1))
                    pool.wait_ge(ln_s1, i + (KT * L + 1))
                    P.tensor_tensor(S1, S1, feature_tile(src, i), ALU.add).then_inc(ln_s1, 1)

            def ln_sub_mean(L, src, scaled):
                pool.wait_ge(ln_rstd, L + 1)

                def sub(kt):
                    s = feature_tile(src, kt)
                    P.tensor_tensor(s, s, MU, ALU.subtract).then_inc(ln_sub, 1)

                def scale(kt, c):
                    pool.wait_ge(ln_h, KT * L + c + 1)
                    P.tensor_scalar(feature_tile(acc, kt), st[:, 3 + c % 2, :], ALPHA, None, ALU.mult).then_inc(ln_scaled, 1)
                sub(0)
                sub(1)
                if scaled:
                    for kt in range(2, KT):
                        sub(kt)
                        scale(kt - 2, kt - 2)
                    scale(14, 14)
                    scale(15, 15)
                else:
                    with pool.Fori(2, KT) as i:
                        sub(i)

            def pool_count(count):
                return count if count < OP_FOX_A else count - OP_FOX_A + OP_FOX_P

            def lanes_free(sem_, count, i=None, step=0):
                pool.wait_ge(sem_, lin(count, i, step))

            def duplicate(dst, n, parts, count, i=None, dc=0):
                for k, (d, s) in enumerate(parts):
                    pool.wait_ge(op_act, lin(count + k + 1, i, dc))
                    if k or count:
                        pool.wait_ge(op_pool, lin(pool_count(count) + k, i, dc))
                    if i is not None:
                        settle(pool)
                    P.tensor_copy(d, s).then_inc(op_pool, 1)

            pool.sem_inc(turned, 2)
            pool.sem_inc(weighed, 2)
            pool.sem_inc(units_begun, 3)
            pool.sem_inc(ln_scaled, 2)
            pool.sem_inc(ln_s1, 1)
            ln_sum(0, acc)
            lanes_free(ln_s1, 1 + KT)
            for k, z in enumerate((sk2[64:128, 0, :].bitcast(f32), sk2[0:64, 1, :].bitcast(f32), sv[64:128, 4, :])):
                P.memset(z, 0.0).then_inc(zeroed_p, 1)
                lanes_free(zeroed_p, k + 1)
            ln_sub_mean(0, acc, False)
            lanes_free(ln_sub, KT)
            cc = slice(CACHE_COL, CACHE_COL + WIN)
            duplicate(sk1, WIN, [(sk1[64:128, 0, cc], sk1[0:64, 0, cc]), (sk1[0:64, 1, cc], sk1[64:128, 1, cc])], 0)
            lanes_free(op_pool, 2)
            pool.wait_ge(ln_h, KT)
            pool.dma_start(f_row(F_C, PAST), t["clogf"]).then_inc(clogf_landed, 16)

            def cosine(r, i=None, dr=0):
                pool.wait_ge(z_ready, lin(r + 1, i, dr))
                P.tensor_tensor(rot[:, :], z_t[:, :], cos_t[:, :], ALU.mult).then_inc(cos_done, 1)
            cosine(0)
            lanes_free(cos_done, 1)
            kk = slice(0, TOK)
            duplicate(sk1, TOK, [(sk1[64:128, 0, kk], sk1[0:64, 0, kk]), (sk1[0:64, 1, kk], sk1[64:128, 1, kk])], 2)
            lanes_free(op_pool, OP_KV)
            pool.wait_ge(rot_ready, 1)
            wait_freed(pool, 1)
            for new, cached, name in ((rot, ck_t, "swa_k"), (va_t, cv_t, "swa_v")):
                pool.dma_start(t[name + "_p"], new[:, PROMPT - WIN:PROMPT]).then_inc(kv_out, 16)
                pool.dma_start(t[name + "_s"][:, 0:WIN - SAMPLE], cached[:, SAMPLE:WIN]).then_inc(kv_out, 16)
                pool.dma_start(t[name + "_s"][:, WIN - SAMPLE:WIN], new[:, PROMPT:TOK]).then_inc(kv_out, 16)
            pool.wait_ge(f_rows, 4)
            pool.dma_start(t["logf"], f_row(F_G, TOK)).then_inc(f_saved, 16)
            for k, (q, kk_, cc_) in enumerate(((F_HI, F_ONE, F_ONE), (F_LO, F_ONE, F_ONE), (F_ONE, F_NHI, F_NHI), (F_ONE, F_NLO, F_NLO))):
                pool.dma_start(t["rows_q"][:, k, :], f_row(q, TOK)).then_inc(f_saved, 16)
                pool.dma_start(t["rows_k"][:, k, :], f_row(kk_, TOK)).then_inc(f_saved, 16)
                pool.dma_start(t["rows_c"][:, k, :], f_row(cc_ if cc_ == F_ONE else cc_ + TOK, PAST)).then_inc(f_saved, 16)
            pool.wait_ge(kv_out, 96)
            pool.wait_ge(op_dve, OP_KV)
            cosine(1)
            pool.wait_ge(f_saved, 16 * 13)

            def cosine_after(r, i=None, dr=0):
                pool.wait_ge(op_dve, lin(OP_KV + 2 * r - 2, i, 2 * dr))
                cosine(r, i, dr)
            with pool.Fori(0, 7) as i:
                cosine_after(2, i, 1)

            pool.wait_ge(out_free, 1 + 2 * PAIRS)
            pool.wait_ge(weighed, 2 + STEPS * PAIRS)
            for k, z in enumerate((*(h for m in (fq2, fk2, fc2) for h in (m[64:128, 0, :].bitcast(f32), m[0:64, 1, :].bitcast(f32))),
                      f_p[:, :, 576:P_COLS], fv[64:128, 4, :])):
                P.memset(z, 0.0).then_inc(zeroed_p, 1)
                lanes_free(zeroed_p, ZERO_SWA + k + 1)

            def fox_pair(q, att, i=None, dp=0):
                dn, df = 3 * dp, 6 * dp

                def dram(tensor, index, n, step):
                    return tensor[index:index + n] if i is None else tensor[bass.ds(i * step + index, n)]
                if att is not None:
                    duplicate(fq2, TOK, [(fq2[0:64, 0, :], fq1[0:64, 0, :]), (fq2[64:128, 1, :], fq1[64:128, 1, :])],
                              OP_FOX_A + 6 * att + 4, i, df)
                    pool.wait_ge(weighed, lin(2 + STEPS * (PAIRS + att), i, STEPS * dp))
                    if i is not None:
                        settle(pool)
                    pool.dma_start(c_v[:, :, :], dram(t["cv"], att, 1, dp).rearrange("o p k c -> p (o k) c")).then_inc(cv_landed, 16)
                if q is None:
                    return
                if q or i is not None:
                    pool.wait_ge(op_dve, lin(OP_FOX_A + 6 * q - 2, i, df))
                if i is not None:
                    settle(pool)
                pool.dma_start(c_t[:, :], dram(t["ck"], q, 1, dp).rearrange("o p c -> p (o c)")).then_inc(ck_landed, 16)
                wait_freed(pool, T_FOX + 3 * q, i, dn)
                if i is not None:
                    settle(pool)
                pool.dma_start(dram(t["fox_v"], q, 1, dp).rearrange("o p c -> p (o c)"), v_t[:, :]).then_inc(v_out, 16)
                pool.wait_ge(scored, lin(STEPS * (PAIRS + q), i, STEPS * dp))
                if i is not None:
                    settle(pool)
                for dst, name in ((fq2, "rows_q"), (fk2, "rows_k"), (fc2, "rows_c")):
                    for head, at in ((0, 64), (1, 0)):
                        pool.dma_start(dst[at:at + 4, head, :].bitcast(f32),
                                       dram(t[name], 2 * q + head, 1, 2 * dp).rearrange("o r c -> (o r) c"))\
                            .then_inc(forget_rows, 16)
                wait_freed(pool, T_FOX + 3 * q + 1, i, dn)
                if i is not None:
                    settle(pool)
                pool.dma_start(dram(t["fox_k"], q, 1, dp).rearrange("o p c -> p (o c)"), k_t[:, :]).then_inc(k_out, 16)
                duplicate(fk1, TOK, [(fk1[64:128, 0, :], fk1[0:64, 0, :]), (fk1[0:64, 1, :], fk1[64:128, 1, :])],
                          OP_FOX_A + 6 * q, i, df)
                duplicate(fc1, PAST, [(fc1[64:128, 0, :], fc1[0:64, 0, :]), (fc1[0:64, 1, :], fc1[64:128, 1, :])],
                          OP_FOX_A + 6 * q + 2, i, df)

            fox_pair(0, None)
            with pool.Fori(0, 3) as i:
                for j in range(2):
                    fox_pair(1 + j, j, i, 2)
            fox_pair(7, 6)
            fox_pair(None, 7)

            lanes_free(op_pool, OP_FOX_P + 6 * PAIRS)
            for c in range(KT):
                pool.wait_ge(y_sum, c + 1)
                P.tensor_scalar(y[:, c, :], y[:, c, :], ALPHA, None, ALU.mult).then_inc(y_ready, 1)
            ln_sum(1, y)
            ln_sub_mean(1, y, True)
            pool.wait_ge(ln_mul, 2 * KT)
            pool.dma_start(p_raw[:, :, :], t["p"]).then_inc(p_landed, 16)
            pool.wait_ge(hid_ready, 64)
            ln_sum(2, acc)
            ln_sub_mean(2, acc, False)

            def store(n, i=None):
                kt = lin(n - T_PG, i, 2)
                pool.wait_ge(gated, lin(n - T_PG + 3, i, 2))
                settle(pool)
                dst = t["y"][n - T_PG:n - T_PG + 1] if i is None else t["y"][bass.ds(kt, 1)]
                pool.dma_start(dst.rearrange("o p c -> p (o c)"), st[:, 2 + n % 2, :]).then_inc(y_out[n % 2], 16)
            with pool.Fori(0, 8) as i:
                for j in range(2):
                    store(T_PG + j, i)
            pool.wait_ge(v_out, 16 * PAIRS)
            pool.wait_ge(k_out, 16 * PAIRS)
            for k in range(2):
                pool.wait_ge(y_out[k], 16 * 8)



def constants():
    import numpy as np
    half = 32
    inv = (np.float32(10000.0) ** (-np.arange(half, dtype=np.float32) / np.float32(half))).astype(np.float32)
    ang = np.arange(TOK, dtype=np.float32)[None, :] * inv[:, None]
    cos, sin = np.cos(ang).astype(np.float32), np.sin(ang).astype(np.float32)
    r = np.arange(128)
    q, k = np.meshgrid(r, np.arange(256), indexing="ij")
    out_of_window = ((q < 64) & (k >= 192)) | ((q >= 64) & (k < 64))
    return {
        "ident": np.eye(128, dtype=np.float32),
        "cos": np.concatenate([cos] * 4), "sin": np.concatenate([-sin, sin] * 2),
        "swap": np.eye(128, dtype=np.float32)[(r // 64) * 64 + (r % 64 + 32) % 64],
        "tri": np.where(r[None, :] > r[:, None], NEG, 0.0).astype(np.float32),
        "win": np.where(out_of_window, NEG, 0.0).astype(np.float32),
    }


def kernel(x_prompt, x_sample, p_prompt, p_sample, cache_swa_k, cache_swa_v, cache_fox_k, cache_fox_v, cache_fox_logf,
           ln0_g, ln0_b, w_in, b_f, sinks, w_o, ln1_g, ln1_b, w_up, w_down, ln2_g, ln2_b, w_pg, b_pg, w_pe):
    import numpy as np
    import concourse.bacc as bacc
    from concourse.bass_utils import run_bass_kernel_spmd

    def arr(a):
        return np.asarray(a)

    def units(w):
        n = w.shape[1] // 128
        return w.reshape(2, 8, 128, n, 128).transpose(3, 0, 2, 1, 4).reshape(2 * n, 128, 1024)

    def by_tile(v):
        return v.reshape(KT, 128).T

    wi = arr(w_in)[0]
    qa, ka, va, qb, kb, vb = (wi[:, a:b] for a, b in ((0, 1024), (1024, 1152), (1152, 1280), (1280, 2304), (2304, 3328), (3328, 4352)))
    qa = qa.reshape(D, 2, 8, 64).transpose(0, 2, 1, 3).reshape(D, 1024)
    fox = np.stack([units(vb).reshape(8, 2, 128, 1024), units(kb).reshape(8, 2, 128, 1024), units(qb).reshape(8, 2, 128, 1024)], 1)
    wo = arr(w_o)[0]
    wo = np.concatenate([wo[:1024].reshape(2, 8, 64, D).transpose(1, 0, 2, 3).reshape(1024, D), wo[1024:]])
    up = units(arr(w_up)[0]).reshape(FF_BLOCKS, 8, 128, 1024)
    down = arr(w_down)[0].reshape(FF_BLOCKS, 4, 128, 8, 256).transpose(0, 3, 2, 1, 4).reshape(FF_BLOCKS, 8, 128, 1024)
    parts = [units(ka), units(va), units(qa), fox.reshape(48, 128, 1024), units(wo), up[0]]
    for k in range(FF_BLOCKS):
        if k + 1 < FF_BLOCKS:
            parts.append(up[k + 1])
        parts.append(down[k])
    parts.append(arr(w_pe)[0].reshape(2, 128, 4, 512).transpose(2, 1, 0, 3).reshape(4, 128, 1024))
    parts.append(units(arr(w_pg)[0]))
    stream = np.concatenate(parts)
    tokens = np.concatenate([arr(x_prompt)[0], arr(x_sample)[0]])
    emb = np.concatenate([arr(p_prompt)[0, 0], arr(p_sample)[0, 0]])
    data = {
        "x": tokens.T.reshape(KT, 128, TOK).transpose(1, 0, 2),
        "w": stream,
        "p": emb.T.reshape(2, 128, TOK).transpose(1, 0, 2),
        "cols": np.concatenate([by_tile(arr(v).reshape(-1)) for v in (ln0_g, ln0_b, ln1_g, ln1_b, ln2_g, ln2_b, b_pg)], 1),
        "sinks": np.broadcast_to(arr(sinks)[0].reshape(2, 8).T.reshape(1, 16), (128, 16)),
        "wf": wi[:, 4352:4368].reshape(KT, 128, 16).transpose(1, 0, 2).reshape(128, 256),
        "bf": arr(b_f)[0].reshape(16, 1),
        "swa_ck": arr(cache_swa_k)[0, 0].reshape(WIN, 128).T,
        "swa_cv_t": arr(cache_swa_v)[0, 0].reshape(WIN, 128).T,
        "swa_cv": arr(cache_swa_v)[0, 0].reshape(WIN, 128),
        "ck": arr(cache_fox_k)[0, 0].reshape(PAST, 8, 128).transpose(1, 2, 0),
        "cv": arr(cache_fox_v)[0, 0].reshape(4, 128, 8, 128).transpose(2, 1, 0, 3),
        "clogf": arr(cache_fox_logf)[0, 0].T,
        **constants(),
    }
    outs = {"y": (KT, 128, TOK), "swa_k_p": (128, WIN), "swa_v_p": (128, WIN), "swa_k_s": (128, WIN), "swa_v_s": (128, WIN),
            "fox_k": (8, 128, TOK), "fox_v": (8, 128, TOK), "logf": (16, TOK)}
    scratch = {"rows_q": (16, 4, TOK), "rows_k": (16, 4, TOK), "rows_c": (16, 4, PAST)}
    nc = bacc.Bacc("TRN2", target_bir_lowering=False, num_devices=1, dynamic_dma_scratch_size=4096)
    f32 = mybir.dt.float32
    data = {f"in_{k}": np.ascontiguousarray(v) for k, v in data.items()}
    t = {k[3:]: nc.dram_tensor(k, v.shape, f32, kind="ExternalInput").ap() for k, v in data.items()}
    t.update({k: nc.dram_tensor(f"out_{k}", v, f32, kind="ExternalOutput").ap() for k, v in outs.items()})
    t.update({k: nc.dram_tensor(k, v, f32, kind="Internal").ap() for k, v in scratch.items()})
    build(nc, t)
    r = run_bass_kernel_spmd(nc, [data], core_ids=[0]).results[0]
    o = {k: r[f"out_{k}"] for k in outs}

    def rows(a, lo, hi):
        return a.reshape(-1, a.shape[-1])[:, lo:hi].T

    def heads(a, lo, hi, n):
        return np.ascontiguousarray(rows(a, lo, hi)).reshape(1, 1, hi - lo, n, 64)

    yt = rows(o["y"], 0, TOK)
    lf = rows(o["logf"], 0, TOK)
    return (np.ascontiguousarray(yt[:PROMPT])[None], np.ascontiguousarray(yt[PROMPT:])[None],
            heads(o["swa_k_p"], 0, WIN, 2), heads(o["swa_v_p"], 0, WIN, 2),
            heads(o["fox_k"], 0, PROMPT, 16), heads(o["fox_v"], 0, PROMPT, 16), np.ascontiguousarray(lf[:PROMPT])[None, None],
            heads(o["swa_k_s"], 0, WIN, 2), heads(o["swa_v_s"], 0, WIN, 2),
            heads(o["fox_k"], PROMPT, TOK, 16), heads(o["fox_v"], PROMPT, TOK, 16), np.ascontiguousarray(lf[PROMPT:])[None, None])
```

```python
import concourse.bass as bass
from concourse import mybir
from contextlib import ExitStack

D = 2048
PROMPT, SAMPLE = 512, 64
TOK = PROMPT + SAMPLE
HALF = TOK // 2
KT = D // 128
PAST = 512
WIN = 128
PAIRS = 8
FF_BLOCKS = 16
EPS = 1e-5
ALPHA = 2.0 ** 0.25
SCALE = 0.125
NEG = -(2.0 ** 100)

RING = 4
U_KV = 0
U_QA = U_KV + 6
U_FOX = U_QA + 2 * PAIRS
U_O = U_FOX + 6 * PAIRS
U_MLP = U_O + 2 * KT
U_PE = U_MLP + 16 * FF_BLOCKS
U_PG = U_PE + 4
UNITS = U_PG + 2 * KT

T_KV = 0
T_QA = T_KV + 3
T_FOX = T_QA + PAIRS
T_O = T_FOX + 3 * PAIRS
T_MLP = T_O + KT
T_PE = T_MLP + 20 * FF_BLOCKS
T_PG = T_PE + KT
IN_MISC = {T_KV: 1024, T_KV + 1: 0, T_MLP + 2: 0, T_MLP + 3: 1024, T_PG + 2: 0, T_PG + 3: 1024}

STEPS = 10
SLOTS = STEPS + 4
SWA_SLOTS = {c: c - 6 for c in range(6, 21)}
FOX_SLOTS = {5 + 3 * j: [j] for j in range(SLOTS)}
F_X, F_M, F_E, F_W, F_L, F_D, F_R, F_G = (TOK * k for k in range(2, 10))
F_SUM = F_G + TOK
F_ALL = TOK + PAST
F_HI = F_X
F_LO = F_HI + F_ALL
F_NHI = F_LO + F_ALL
F_NLO = F_SUM + F_ALL
F_C = F_NLO + F_ALL
F_ONE = F_C + PAST
N_CONSTS = 12
CACHE_COL = TOK
P_COLS = PAST + SAMPLE


LAST_SLOTS = {5: [0, 1], **{c: [c - 4] for c in range(6, 15)}, 15: [11, 12, 13]}


def lin(const, i, step):
    return const if i is None else i * step + const


class Chain:

    def __init__(self, eng, sem):
        self.eng, self.sem, self.n, self.i, self.step, self.start = eng, sem, 0, None, 0, 0

    def add(self, ins):
        ins.then_inc(self.sem, 1)
        self.n += 1
        return ins

    def wait(self, back=0):
        self.eng.wait_ge(self.sem, lin(self.n - back, self.i, self.step))

    def enter(self, i, step):
        self.i, self.step, self.start = i, step, self.n

    def leave(self, count):
        assert self.n - self.start == self.step, (self.n - self.start, self.step)
        self.n, self.i = self.start + self.step * count, None


class Ahead:

    def __init__(self, split):
        self.split, self.next = split, 0

    def upto(self, u, i=None, du=0):
        while self.next <= min(u, UNITS - 1):
            self.split(self.next, i, du)
            self.next += 1

    def leave(self, count, du):
        self.next += du * (count - 1)


def feature_tile(tensor, kt):
    if isinstance(kt, int):
        return tensor[:, kt, :]
    return tensor[:, bass.ds(kt, 1), :].rearrange("p o t -> p (o t)")


def halves(ap):
    return ap.rearrange("p (a b) -> p a b", a=2)


def freed(n):
    return n % 2, n // 2 + 2


def step_of(s):
    return (s // 4, s % 4) if s < 8 else (s - 8, 4)



def span(kind, j):
    head, qt = step_of(j)
    if kind == "swa":
        return 512 * (j % 2), 1 + (128 if qt == 0 else 256 if qt < 4 else WIN + SAMPLE)
    return (512 * (j % 2), 128 * (qt + 1)) if qt < 4 else (0, PAST + SAMPLE)


def turn_width(kind, qt):
    if kind == "swa":
        return 128 if qt == 0 else 256 if qt < 4 else 128
    return 128 * (qt + 1) if qt < 4 else 5 * SAMPLE


def build(nc, t):
    f32, f32r = mybir.dt.float32, mybir.dt.float32r
    ACT, ALU = mybir.ActivationFunctionType, mybir.AluOpType
    AX = mybir.AxisListType.X
    outer = ExitStack()
    with outer:
        def sb(name, shape, dt=f32, scope=outer):
            return scope.enter_context(nc.sbuf_tensor(name, shape, dt))

        def sem(name):
            return outer.enter_context(nc.semaphore(name))

        x_hi = sb("x_hi", [128, KT, TOK], f32r)
        x_lo = sb("x_lo", [128, KT, TOK], f32r)
        acc = sb("acc", [128, KT, TOK])
        w_raw = sb("w_raw", [128, RING, 1024])
        w_hi = sb("w_hi", [128, RING, 1024], f32r)
        w_lo = sb("w_lo", [128, RING, 1024], f32r)
        ident_r = sb("ident_r", [128, 128], f32r)
        ident = ident_r.bitcast(f32)
        tri_r = sb("tri_r", [128, 128], f32r)
        mean_w = sb("mean_w", [128, 128])
        cols = sb("cols", [128, 7 * KT])
        stat = sb("stat", [128, 3, 3])
        st = sb("st", [128, 5, TOK])
        S1, S2, SH, WK = (st[:, k, :] for k in range(4))
        WK2 = st[:, 4, :]
        MU, VAR, RSTD = S1, S2, SH

        swa = ExitStack()
        win_r = sb("win_r", [128, 256], f32r, swa)
        sinks = sb("sinks", [128, 2 * PAIRS], f32, swa)
        sk1 = sb("sk1", [128, 2, TOK + WIN], f32r, swa)
        sk2 = sb("sk2", [128, 2, TOK + WIN], f32r, swa)
        sq1 = sb("sq1", [128, 2, TOK], f32r, swa)
        sv = sb("sv", [128, 6, 128], f32, swa)
        s_p = sb("s_p", [128, 4, 2 * 128 + 1], f32, swa)
        s_pt = sb("s_pt", [128, 2, 256], f32, swa)
        cos_t = sb("cos_t", [128, TOK], f32, swa)
        sin_t = sb("sin_t", [128, TOK], f32, swa)
        swap = sb("swap", [128, 128], f32, swa)
        win_f = sb("win_f", [128, 256], f32, swa)
        tri_f = sb("tri_f", [128, 128], f32, swa)
        ident_f = sb("ident_f", [128, 128], f32, swa)
        bf = sb("bf", [16, 1], f32, swa)
        z_t = sb("z_t", [128, TOK], f32, swa)
        rot = sb("rot", [128, TOK], f32, swa)
        rot2 = sb("rot2", [128, TOK], f32, swa)
        k_rot = sb("k_rot", [128, TOK], f32, swa)
        va_t = sb("va_t", [128, TOK], f32, swa)
        ck_t = sb("ck_t", [128, WIN], f32, swa)
        cv_t = sb("cv_t", [128, WIN], f32, swa)
        swa.close()

        fox = ExitStack()
        fq1 = sb("fq1", [128, 2, TOK], f32r, fox)
        fq2 = sb("fq2", [128, 2, TOK], f32r, fox)
        fv = sb("fv", [128, 5, 128], f32, fox)
        c_v = sb("c_v", [128, 4, 128], f32, fox)
        f_p = sb("f_p", [128, 4, P_COLS], f32, fox)
        f_pt = sb("f_pt", [128, 2, 512], f32, fox)
        v_t = sb("v_t", [128, TOK], f32, fox)
        k_t = sb("k_t", [128, TOK], f32, fox)
        c_t = sb("c_t", [128, PAST], f32, fox)
        fk1 = sb("fk1", [128, 2, TOK], f32r, fox)
        fk2 = sb("fk2", [128, 2, TOK], f32r, fox)
        fc1 = sb("fc1", [128, 2, PAST], f32r, fox)
        fc2 = sb("fc2", [128, 2, PAST], f32r, fox)
        fox.close()

        late = ExitStack()
        p_raw = sb("p_raw", [128, 2, TOK], f32, late)
        p_hi = sb("p_hi", [128, 2, TOK], f32r, late)
        p_lo = sb("p_lo", [128, 2, TOK], f32r, late)
        mlp = ExitStack()
        hid_hi = sb("hid_hi", [128, 2, 4, TOK], f32r, mlp)
        hid_lo = sb("hid_lo", [128, 2, 4, TOK], f32r, mlp)
        mlp.close()
        pe_out = sb("pe_out", [128, KT, TOK], f32, late)
        late.close()

        tiles_ps = [outer.enter_context(nc.psum_tensor(f"tile{k}", [128, 2, 512], f32)) for k in range(2)]
        misc = outer.enter_context(nc.psum_tensor("misc", [128, 2048], f32))
        scores_ps, turn_ps, out_ps = misc[:, 0:1024], misc[:, 1024:1536], misc[:, 1536:2048]

        def misc_halves(first):
            return misc[:, first:first + 1024].rearrange("p (a b) -> p a b", a=2)[:, :, 0:HALF]

        def tile_ps(n):
            return misc_halves(IN_MISC[n]) if n in IN_MISC else tiles_ps[n % 2][:, :, 0:HALF]

        x_landed = [sem(f"x_landed{k}") for k in range(4)]
        consts = sem("consts")
        settled = sem("settled")
        w_landed = [sem(f"w_landed{k}") for k in range(RING)]
        w_hi_done = sem("w_hi_done")
        w_split = sem("w_split")
        units_begun = sem("units_begun")
        tile_done = sem("tile_done")
        tile_free = [sem(f"tile_free{k}") for k in range(2)]
        masks = sem("masks")
        zeroed_p, zeroed_v = sem("zeroed_p"), sem("zeroed_v")
        ln_cent, ln_sq, ln_s1, ln_s2 = sem("ln_cent"), sem("ln_sq"), sem("ln_s1"), sem("ln_s2")
        ln_mm, ln_sd, ln_rstd = sem("ln_mm"), sem("ln_sd"), sem("ln_rstd")
        ln_var, ln_log = sem("ln_var"), sem("ln_log")
        keys_out, va_out = sem("keys_out"), sem("va_out")
        ln_sub, ln_mul, ln_h, ln_scaled = sem("ln_sub"), sem("ln_mul"), sem("ln_h"), sem("ln_scaled")
        x_hi_done, x_ready = sem("x_hi_done"), sem("x_ready")
        z_ready, swapped, cos_done, rot_ready = sem("z_ready"), sem("swapped"), sem("cos_done"), sem("rot_ready")
        op_act, op_dve, op_pool = sem("op_act"), sem("op_dve"), sem("op_pool")
        va_turned, sv_ready = sem("va_turned"), sem("sv_ready")
        kv_out = sem("kv_out")
        f_exp, f_arg, f_log, f_w, f_sum, f_hi, f_rows, f_saved = (sem(n) for n in (
            "f_exp", "f_arg", "f_log", "f_w", "f_sum", "f_hi", "f_rows", "f_saved"))
        clogf_landed = sem("clogf_landed")
        scored = sem("scored")
        negmax = sem("negmax")
        exp_done = sem("exp_done")
        normed = sem("normed")
        turned = sem("turned")
        turn_out = sem("turn_out")
        weighed = sem("weighed")
        out_free = sem("out_free")
        v_turned, fv_ready = sem("v_turned"), sem("fv_ready")
        v_out, k_out, forget_rows = sem("v_out"), sem("k_out"), sem("forget_rows")
        ck_landed, cv_landed = sem("ck_landed"), sem("cv_landed")
        hsq_done, hid_hi_done, hid_ready = sem("hsq_done"), sem("hid_hi_done"), sem("hid_ready")
        y_sum, y_ready = sem("y_sum"), sem("y_ready")
        p_landed, p_hi_done, p_ready = sem("p_landed"), sem("p_hi_done"), sem("p_ready")
        gated = sem("gated")
        y_out = [sem("y_out0"), sem("y_out1")]
        ch_dve, ch_pool = sem("ch_dve"), sem("ch_pool")

        OP_KV = 4
        OP_FOX_A = OP_KV + 2 * PAIRS
        OP_FOX_P = OP_KV

        def wait_freed(eng, n, i=None, dn=0):
            k, count = freed(n)
            eng.wait_ge(tile_free[k], lin(count, i, dn // 2))

        def sink_col(pair, head, i, dp):
            if i is None:
                return sinks[:, 2 * pair + head:2 * pair + head + 1]
            return sinks[:, bass.ds(i * (2 * dp) + (2 * pair + head), 1)]

        def settle(eng):
            eng.sem_inc(settled, 1)

        block = outer.enter_context(nc.Block())

        ZERO_SWA, ZERO_ALL = 2, 2 + 6
        f_tmp = acc[0:16, :, :].rearrange("p k t -> p (k t)")

        def f_row(col, n):
            return f_tmp[:, col:col + n]

        @block.sync
        def _(sp):
            for k in range(4):
                sp.dma_start(acc[:, 4 * k:4 * k + 4, :], t["x"][:, 4 * k:4 * k + 4, :]).then_inc(x_landed[k], 16)
            def fetch(u, s):
                sp.wait_ge(w_split, u + 1)
                unit = t["w"][u:u + 1] if isinstance(u, int) else t["w"][bass.ds(u, 1)]
                sp.dma_start(w_raw[:, s, :], unit.rearrange("o p c -> p (o c)")).then_inc(w_landed[s], 16)
            with sp.Fori(0, UNITS // RING) as r:
                for s in range(RING):
                    fetch(r * RING + s, s)
            for u in range(UNITS // RING * RING, UNITS):
                fetch(u, u % RING)

        @block.tensor
        def _(pe):
            def products(dst, hi, lo, xh, xl, first, last, begin=False):
                ins = None
                for a, (w, x) in enumerate(((hi, xh), (hi, xl), (lo, xh))):
                    for h in range(2):
                        ins = nc.tensor.matmul(dst[:, h, :], w, x[:, h * HALF:(h + 1) * HALF],
                                               start=first and a == 0, stop=last and a == 2)
                        if begin and a == 0 and h == 0:
                            ins.then_inc(units_begun, 1)
                return ins

            def tile(n, u, i=None, dn=0, du=0, x_gen=None, between=None, c0=0):
                wait_freed(pe, n - 2, i, dn)
                for c in range(KT):
                    if between:
                        between(c0 + c)
                    if c % 8 == 0:
                        pe.wait_ge(w_split, lin(RING + u + c // 8 + 1, i, du))
                    if x_gen is not None:
                        pe.wait_ge(x_ready, 2 + KT * x_gen + c + 1)
                    slot = (u + c // 8) % RING
                    cut = slice(128 * (c % 8), 128 * (c % 8) + 128)
                    ins = products(tile_ps(n), w_hi[:, slot, cut], w_lo[:, slot, cut], x_hi[:, c, :], x_lo[:, c, :],
                                   c == 0, c == KT - 1, begin=c % 8 == 0)
                ins.then_inc(tile_done, 1)

            def quad(n, u, x_gen, widths=(128,) * 4):
                if n:
                    wait_freed(pe, n - 2)
                    wait_freed(pe, n - 1)
                for c in range(KT):
                    if c % 2 == 0:
                        pe.wait_ge(w_split, RING + u + c // 2 + 1)
                    pe.wait_ge(x_ready, 2 + KT * x_gen + c + 1)
                    slot = (u + c // 2) % RING
                    for j, width in enumerate(widths):
                        at = 512 * (c % 2) + 128 * j
                        ins = products(tile_ps(n + j)[0:width], w_hi[:, slot, at:at + width], w_lo[:, slot, at:at + width],
                                       x_hi[:, c, :], x_lo[:, c, :], c == 0, c == KT - 1, begin=c % 2 == 0 and j == 0)
                        if c == KT - 1:
                            ins.then_inc(tile_done, 1)

            def down_unit(n, u, hs, i=None, dn=0, du=0, between=None):
                pe.wait_ge(w_split, lin(RING + u + 1, i, du))
                slot = u % RING
                for j in range(2):
                    wait_freed(pe, n + j - 2, i, dn)
                    for k in range(4):
                        cut = slice(256 * k + 128 * j, 256 * k + 128 * j + 128)
                        ins = products(tile_ps(n + j), w_hi[:, slot, cut], w_lo[:, slot, cut], hid_hi[:, hs, k, :],
                                       hid_lo[:, hs, k, :], k == 0, k == 3, begin=j == 0 and k == 0)
                    ins.then_inc(tile_done, 1)

            def ln_shift(src):
                for h in range(2):
                    ins = nc.tensor.matmul(misc_halves(0)[:, h, :], mean_w[:, :], halves(src)[:, h, :], start=True, stop=True)
                ins.then_inc(ln_mm, 1)

            def ln_sums(L):
                pe.wait_ge(ln_s1, 1 + KT * (L + 1))
                pe.wait_ge(ln_s2, 1 + KT * (L + 1))
                for k, s in enumerate((S1, S2)):
                    for h in range(2):
                        ins = nc.tensor.matmul(misc_halves(1024 * k)[:, h, :], mean_w[:, :], halves(s)[:, h, :],
                                               start=True, stop=True)
                ins.then_inc(ln_mm, 1)

            def attend(kind, j, pair, i=None, dp=0):
                g0, dg = STEPS * pair, STEPS * dp
                q1, k1, k2 = (sq1, sk1, sk2) if kind == "swa" else (fq1, fk1, fk2)
                p, pt = (s_p, s_pt) if kind == "swa" else (f_p, f_pt)
                if j < STEPS:
                    head, qt = step_of(j)
                    if j == 0:
                        pe.wait_ge(out_free, lin(2 * pair + 1, i, 2 * dp))
                    both = kind == "fox" and qt == 4
                    pe.wait_ge(exp_done, lin(g0 + j + (2 if both else 1), i, dg))
                    lhs = slice(128 * qt, 128 * qt + 128) if qt < 4 else slice(TOK - 128, TOK)
                    ins = None

                    def score(at, width, ka, kb, key, mask=None):
                        dst = scores_ps[:, at:at + width]
                        qb = q1 if kind == "swa" else fq2
                        nc.tensor.matmul(dst, q1[:, head, lhs], ka[:, head, key:key + width], start=True, stop=False)
                        last = nc.tensor.matmul(dst, qb[:, head, lhs], kb[:, head, key:key + width], start=False,
                                                stop=mask is None)
                        if mask is not None:
                            m, mw = mask
                            last = nc.tensor.matmul(scores_ps[:, at + width - mw:at + width], ident_r[:, :], m,
                                                    start=False, stop=True)
                        return last
                    at = 512 * (j % 2)
                    if kind == "swa":
                        if qt == 0:
                            score(at, 128, k1, k2, 0, (win_r[:, 128:256], 128))
                        elif qt < 4:
                            score(at, 256, k1, k2, 128 * (qt - 1), (win_r[:, :], 256))
                        else:
                            score(at, 128, k1, k2, CACHE_COL)
                            score(at + WIN, SAMPLE, k1, k2, PROMPT)
                        end = at + span(kind, j)[1]
                        ins = nc.tensor.matmul(scores_ps[:, end - 1:end], ident[:, :], sink_col(pair, head, i, dp),
                                               start=True, stop=True)
                    else:
                        if qt < 4:
                            ins = score(at, 128 * (qt + 1), k1, k2, 0, (tri_r[:, :], 128))
                        else:
                            score(0, PAST, fc1, fc2, 0)
                            ins = score(512, SAMPLE, k1, k2, PROMPT, (tri_r[:, 64:128], SAMPLE))
                    ins.then_inc(scored, 1)
                if 3 <= j <= STEPS + 2:
                    s = j - 3
                    head, qt = step_of(s)
                    pe.wait_ge(normed, lin(g0 + s + 1, i, dg))
                    pe.wait_ge(turn_out, lin(g0 + s + 1, i, dg))
                    if qt == 4 and i is not None:
                        settle(pe)
                    cols_ = key_cols(kind, qt)
                    for k, col in enumerate(cols_):
                        if qt < 4:
                            ins = nc.tensor.transpose(turn_ps[:, 128 * k:128 * k + 128], p[:, s % 4, col:col + 128], ident[:, :])
                        else:
                            keys = SAMPLE if k == len(cols_) - 1 else 128
                            ins = nc.tensor.transpose(turn_ps[0:keys, 64 * k:64 * k + 64], p[64:128, s % 4, col:col + keys],
                                                      ident[64:128, 64:128])
                    ins.then_inc(turned, 1)
                if j >= 4:
                    s = j - 4
                    head, qt = step_of(s)
                    pe.wait_ge(turn_out, lin(g0 + s + 2, i, dg))
                    if s == 8:
                        pe.wait_ge(exp_done, lin(g0 + STEPS + 2, i, dg))
                    if s == 8 and kind == "fox":
                        pe.wait_ge(cv_landed, lin(16 * (pair - PAIRS) + 16, i, 16 * dp))
                    width = 128 if qt < 4 else SAMPLE
                    dst = out_ps[64 * head:64 * head + 64, 128 * qt:128 * qt + 128] if qt < 4 else \
                        scores_ps[64 * head:64 * head + 64, 512 - SAMPLE:512]
                    vals = value_tiles(kind, qt)
                    for k, (vt, at) in enumerate(vals):
                        keys = SAMPLE if qt == 4 and k == len(vals) - 1 else 128
                        ins = nc.tensor.matmul(dst, vt[0:keys, at, 64 * head:64 * head + 64],
                                               pt[0:keys, s % 2, width * k:width * k + width],
                                               start=k == 0, stop=k == len(vals) - 1)
                    ins.then_inc(weighed, 1)

            def key_cols(kind, qt):
                if kind == "swa":
                    return [0] if qt == 0 else [0, 128]
                return [128 * k for k in range(qt + 1)]

            def value_tiles(kind, qt):
                if kind == "swa":
                    return [(sv, 0)] if qt == 0 else [(sv, qt - 1), (sv, qt)] if qt < 4 else [(sv, 5), (sv, 4)]
                return [(fv, k) for k in range(qt + 1)] if qt < 4 else [(c_v, k) for k in range(4)] + [(fv, 4)]

            def turn_values(src):
                for k in range(4):
                    nc.tensor.transpose(scores_ps[:, 128 * k:128 * k + 128], src[:, 128 * k:128 * k + 128], ident[:, :])
                return nc.tensor.transpose(scores_ps[0:64, 512:640], src[:, 512:576], ident[:, :])

            pe.wait_ge(x_landed[0], 16)
            pe.wait_ge(zeroed_v, 1)
            ln_shift(acc[:, 0, :])
            pe.wait_ge(consts, 16 * N_CONSTS)
            ln_sums(0)
            quad(T_KV, U_KV, 0, (128, 128, 16, 128))

            def rotate(r, n, i=None, dr=0):
                pe.wait_ge(z_ready, lin(r + 1, i, dr))
                for h in range(2):
                    ins = nc.tensor.matmul(tile_ps(n)[:, h, :], swap[:, :], z_t[:, h * HALF:(h + 1) * HALF], start=True, stop=True)
                ins.then_inc(swapped, 1)

            def swa_between(c, pair, i=None, dp=0):
                if pair:
                    swa_rest(c, pair - 1, i, dp)
                if c == 1:
                    rotate(pair + 1, T_QA + pair, i, dp)
                if c == 6:
                    pe.wait_ge(op_dve, lin(OP_KV + 2 * pair + 2, i, 2 * dp))
                if c >= 6:
                    attend("swa", SWA_SLOTS[c], pair, i, dp)

            def swa_rest(c, pair, i=None, dp=0):
                if SWA_SLOTS.get(KT + c, SLOTS) < SLOTS:
                    attend("swa", SWA_SLOTS[KT + c], pair, i, dp)

            def swa_keys_ready():
                pe.wait_ge(op_dve, OP_KV)
                pe.wait_ge(op_pool, OP_KV)
                pe.wait_ge(zeroed_p, ZERO_SWA)
                pe.wait_ge(sv_ready, 2)
                pe.wait_ge(masks, 3)

            def first_between(c):
                if c == 1:
                    rotate(0, T_KV)
                    pe.wait_ge(va_out, 1)
                    turn_values(va_t).then_inc(va_turned, 1)
                if c == 3:
                    rotate(1, T_QA)
                if c == 6:
                    swa_keys_ready()
                if c >= 6:
                    swa_between(c, 0)
            tile(T_QA + 1, U_QA + 2, between=first_between)
            with pe.Fori(0, 3) as i:
                for j in range(2):
                    tile(T_QA + 2 + j, U_QA + 4 + 2 * j, i, 2, 4, between=lambda c, j=j: swa_between(c, 1 + j, i, 2))

            def fox_between(c, q, i=None, dp=0, slots=FOX_SLOTS):
                pair = PAIRS + q
                if c == 2:
                    wait_freed(pe, T_FOX + 3 * q, i, 3 * dp)
                    pe.wait_ge(exp_done, lin(STEPS * pair + 2, i, STEPS * dp))
                    pe.wait_ge(out_free, lin(2 * pair + 1, i, 2 * dp))
                    turn_values(v_t).then_inc(v_turned, 1)
                if c == 5:
                    pe.wait_ge(fv_ready, lin(2 * q + 2, i, 2 * dp))
                    pe.wait_ge(op_dve, lin(OP_FOX_A + 6 * q + 6, i, 6 * dp))
                    pe.wait_ge(op_pool, lin(OP_FOX_P + 6 * q + 6, i, 6 * dp))
                    pe.wait_ge(forget_rows, lin(96 * q + 96, i, 96 * dp))
                    pe.wait_ge(zeroed_p, ZERO_ALL)
                for j in slots.get(c, ()):
                    attend("fox", j, pair, i, dp)

            def fox_tiles(q, att, i=None, dp=0):
                for k in range(3):
                    tile(T_FOX + 3 * q + k, U_FOX + 6 * q + 2 * k, i, 3 * dp, 6 * dp,
                         between=lambda c: fox_between(c, att, i, dp), c0=KT * k)

            tile(T_FOX, U_FOX, between=lambda c: swa_between(c, PAIRS - 1))
            tile(T_FOX + 1, U_FOX + 2, between=lambda c: swa_rest(c, PAIRS - 1))
            tile(T_FOX + 2, U_FOX + 4)
            with pe.Fori(0, 3) as i:
                for j in range(2):
                    fox_tiles(1 + j, j, i, 2)
            fox_tiles(7, 6)

            wait_freed(pe, T_O - 2)
            wait_freed(pe, T_O - 1)
            for c in range(KT):
                fox_between(c, 7, slots=LAST_SLOTS)
                if c % 4 == 0:
                    pe.wait_ge(w_split, RING + U_O + c // 4 + 1)
                pe.wait_ge(x_ready, 2 + KT + c + 1)
                slot = (U_O + c // 4) % RING
                for j in range(2):
                    at = 256 * (c % 4) + 128 * j
                    ins = products(tile_ps(T_O + j), w_hi[:, slot, at:at + 128], w_lo[:, slot, at:at + 128],
                                   x_hi[:, c, :], x_lo[:, c, :], c == 0, c == KT - 1, begin=c % 4 == 0 and j == 0)
                    if c == KT - 1:
                        ins.then_inc(tile_done, 1)

            def first_shift(c):
                if c == 2:
                    wait_freed(pe, T_O)
                    ln_shift(acc[:, 0, :])
            tile(T_O + 2, U_O + 4, between=first_shift)
            tile(T_O + 3, U_O + 6)
            with pe.Fori(0, 6) as i:
                for j in range(2):
                    tile(T_O + 4 + j, U_O + 8 + 2 * j, i, 2, 4)
            ln_sums(1)

            def up(n, u, i=None, dn=0, du=0):
                for k in range(4):
                    tile(n + k, u + 2 * k, i, dn, du)

            def down(n, u, fb, i=None, dn=0, du=0, df=0):
                pe.wait_ge(hid_ready, lin(4 * fb + 4, i, 4 * df))
                for k in range(8):
                    down_unit(n + 2 * k, u + k, fb % 2, i, dn, du)

            quad(T_MLP, U_MLP, 2)
            with pe.Fori(0, 7) as i:
                for j in range(2):
                    up(T_MLP + 4 + 20 * j, U_MLP + 8 + 16 * j, i, 40, 32)
                    down(T_MLP + 8 + 20 * j, U_MLP + 16 + 16 * j, j, i, 40, 32, 2)
            up(T_MLP + 284, U_MLP + 232)
            down(T_MLP + 288, U_MLP + 240, 14)
            pe.wait_ge(hid_ready, 64)
            for k in range(8):
                if k == 1:
                    wait_freed(pe, T_MLP + 304)
                    ln_shift(acc[:, 0, :])
                down_unit(T_MLP + 304 + 2 * k, U_MLP + 248 + k, 1)

            pe.wait_ge(p_ready, 1)
            for u in range(4):
                slot = (U_PE + u) % RING
                pe.wait_ge(w_split, RING + U_PE + u + 1)
                for j in range(4):
                    n = T_PE + 4 * u + j
                    wait_freed(pe, n - 2)
                    for k in range(2):
                        cut = slice(512 * k + 128 * j, 512 * k + 128 * j + 128)
                        ins = products(tile_ps(n), w_hi[:, slot, cut], w_lo[:, slot, cut], p_hi[:, k, :], p_lo[:, k, :],
                                       k == 0, k == 1, begin=j == 0 and k == 0)
                    ins.then_inc(tile_done, 1)
                if u == 1:
                    ln_sums(2)
            quad(T_PG, U_PG, 3)
            with pe.Fori(0, 6) as i:
                for j in range(2):
                    tile(T_PG + 4 + j, U_PG + 8 + 2 * j, i, 2, 4)

        @block.scalar
        def _(act):
            def copy(out, in_, scale=1.0, func=ACT.Copy):
                return nc.scalar.activation(out, in_, func, scale=scale)

            def split(u, i, du):
                act.wait_ge(w_landed[u % RING], lin(16 * (u // RING) + 16, i, 4 * du))
                act.wait_ge(units_begun, lin(u + 1, i, du))
                copy(w_hi[:, u % RING, :], w_raw[:, u % RING, :]).then_inc(w_hi_done, 1)
            ahead = Ahead(split)

            def ln_square(L, c, src):
                act.wait_ge(ln_cent, c + KT * L + 1)
                act.wait_ge(ln_s2, c + KT * L + 1)
                nc.scalar.activation(WK, src, ACT.Square).then_inc(ln_sq, 1)

            def ln_root(L):
                act.wait_ge(ln_var, L + 1)
                nc.scalar.activation(WK, VAR, ACT.Ln).then_inc(ln_log, 1)
                act.wait_ge(ln_log, L + 1)
                nc.scalar.activation(RSTD, WK, ACT.Exp, scale=-0.5).then_inc(ln_sd, 1)

            def ln_apply(L, gen, src, scaled, u):
                act.wait_ge(ln_rstd, L + 1)
                for c in range(KT):
                    if c % 2 == 0:
                        ahead.upto(u + 1 + c // 2)
                    work = st[:, 3 + c % 2, :]
                    act.wait_ge(ln_mul, KT * L + c + 1)
                    act.wait_ge(x_ready, KT * gen + c + 1)
                    if scaled:
                        act.wait_ge(ln_scaled, c + 1)
                    g, b = 2 * L * KT + c, (2 * L + 1) * KT + c
                    nc.scalar.activation(work, src[:, c, :], ACT.Identity, bias=cols[:, b:b + 1], scale=cols[:, g:g + 1])\
                        .then_inc(ln_h, 1)
                    act.wait_ge(ln_h, KT * L + c + 1)
                    copy(x_hi[:, c, :], work).then_inc(x_hi_done, 1)

            def attend(kind, j, pair, i=None, dp=0):
                g0, dg = STEPS * pair, STEPS * dp
                p, pt = (s_p, s_pt) if kind == "swa" else (f_p, f_pt)
                if j < STEPS:
                    head, qt = step_of(j)
                    act.wait_ge(negmax, lin(g0 + j + 1, i, dg))
                    act.wait_ge(turned, lin(g0 + 2 + max(0, j - 3), i, dg))
                    at, width = span(kind, j)
                    s = j % 3
                    nc.scalar.activation(p[:, j % 4, 0:width], scores_ps[:, at:at + width], ACT.Exp,
                                         bias=stat[:, s, 0:1], scale=1.0, accum_out=stat[:, s, 1:2]).then_inc(exp_done, 1)
                if 3 <= j <= STEPS + 2:
                    s = j - 3
                    head, qt = step_of(s)
                    act.wait_ge(turned, lin(g0 + s + 3, i, dg))
                    act.wait_ge(weighed, lin(g0 + s + 1, i, dg))
                    width = turn_width(kind, qt)
                    copy(pt[:, s % 2, 0:width], turn_ps[:, 0:width]).then_inc(turn_out, 1)
                if j in (12, 14):
                    act.wait_ge(weighed, lin(g0 + 2 + (8 if j == 12 else 10), i, dg))
                    kt = lin(pair, i, dp)
                    dst = feature_tile(acc, kt)
                    if j == 12:
                        copy(dst[:, 0:PROMPT], out_ps[:, :]).then_inc(out_free, 1)
                    else:
                        copy(dst[:, PROMPT:TOK], scores_ps[:, 512 - SAMPLE:512]).then_inc(out_free, 1)

            act.sem_inc(exp_done, 2)
            act.sem_inc(turn_out, 1)
            act.sem_inc(out_free, 1)
            for dst, name in ((ident_f, "ident"), (cols, "cols"), (cos_t, "cos"), (sin_t, "sin"), (swap, "swap"), (win_f, "win"),
                              (tri_f, "tri"), (sinks, "sinks"), (bf, "bf"), (ck_t, "swa_ck"), (cv_t, "swa_cv_t")):
                act.dma_start(dst[:, :], t[name]).then_inc(consts, 16)
            act.dma_start(sv[:, 5, :], t["swa_cv"]).then_inc(consts, 16)
            for c in range(KT):
                ln_square(0, c, acc[:, c, :])
            ahead.upto(1)
            act.wait_ge(consts, 16 * N_CONSTS)
            copy(ident_r[:, :], ident_f[:, :]).then_inc(masks, 1)
            copy(tri_r[:, :], tri_f[:, :]).then_inc(masks, 1)
            copy(win_r[:, :], win_f[:, :]).then_inc(masks, 1)
            ln_root(0)
            ln_apply(0, 0, acc, False, U_KV)

            def window(dst, src, n):
                copy(dst[0:64, 0, n[0]:n[1]], src[0:64, :], SCALE if dst is sq1 else 1.0).then_inc(op_act, 1)
                copy(dst[64:128, 1, n[0]:n[1]], src[64:128, :], SCALE if dst is sq1 else 1.0).then_inc(op_act, 1)

            window(sk1, ck_t, (CACHE_COL, CACHE_COL + WIN))
            act.wait_ge(tile_done, 1)
            copy(halves(z_t[:, :]), tile_ps(T_KV)).then_inc(z_ready, 1)
            act.wait_ge(tile_done, 2)
            copy(halves(va_t[:, :]), tile_ps(T_KV + 1)).then_inc(va_out, 1)
            ahead.upto(U_KV + 9)
            act.wait_ge(rot_ready, 1)
            window(sk1, k_rot, (0, TOK))
            act.wait_ge(va_turned, 1)
            copy(sv[:, 0:4, :], scores_ps[:, 0:512].rearrange("p (a b) -> p a b", a=4)).then_inc(sv_ready, 1)
            copy(sv[0:64, 4, :], scores_ps[0:64, 512:640]).then_inc(sv_ready, 1)

            def gates(c):
                if c == 6:
                    act.wait_ge(f_arg, 1)
                    nc.scalar.activation(f_tmp[:, F_E:F_E + TOK], f_tmp[:, F_X:F_X + TOK], ACT.Exp, scale=-1.0).then_inc(f_exp, 1)
                if c == 8:
                    act.wait_ge(f_w, 1)
                    nc.scalar.activation(f_tmp[:, F_L:F_L + TOK], f_tmp[:, F_W:F_W + TOK], ACT.Ln).then_inc(f_log, 1)
                if c == 14:
                    act.wait_ge(f_sum, 1)
                    copy(f_tmp.bitcast(f32r)[:, F_HI:F_HI + TOK + PAST], f_tmp[:, F_SUM:F_SUM + TOK + PAST]).then_inc(f_hi, 1)

            def swa_part(c, att, i=None, dp=0):
                if c == 1:
                    act.wait_ge(tile_done, lin(T_QA + att + 1, i, dp))
                    act.wait_ge(swapped, lin(att + 1, i, dp))
                    act.wait_ge(cos_done, lin(att + 1, i, dp))
                    copy(halves(z_t[:, :]), tile_ps(T_QA + att)).then_inc(z_ready, 1)
                if KT + c in SWA_SLOTS and att:
                    attend("swa", SWA_SLOTS[KT + c], att - 1, i, dp)
                if c == 2:
                    act.wait_ge(rot_ready, lin(att + 2, i, dp))
                    window(sq1, rot, (0, TOK))
                if c in SWA_SLOTS:
                    attend("swa", SWA_SLOTS[c], att, i, dp)

            def swa_pair(q, att, i=None, dp=0):
                for c in range(KT):
                    if c % 8 == 0:
                        ahead.upto(U_QA + 2 * q + c // 8 + 2, i, 2 * dp)
                    swa_part(c, att, i, dp)
                    if q == 1:
                        gates(c)

            swa_pair(1, 0)
            act.wait_ge(f_saved, 16 * 13)
            with act.Fori(0, 3) as i:
                for j in range(2):
                    swa_pair(2 + j, 1 + j, i, 2)
            ahead.leave(3, 4)

            def own(dst, src, n, scale=1.0):
                copy(dst[0:64, 0, 0:n], src[0], scale).then_inc(op_act, 1)
                copy(dst[64:128, 1, 0:n], src[1], scale).then_inc(op_act, 1)

            def fox_queries(att, i=None, dp=0):
                act.wait_ge(tile_done, lin(T_FOX + 3 * att + 3, i, 3 * dp))
                ps = tile_ps(T_FOX + 3 * att + 2)
                copy(halves(fq1[0:64, 0, :]), ps[0:64], SCALE).then_inc(op_act, 1)
                copy(halves(fq1[64:128, 1, :]), ps[64:128], SCALE).then_inc(op_act, 1)

            def fox_values(att, i=None, dp=0):
                act.wait_ge(v_turned, lin(att + 1, i, dp))
                copy(fv[:, 0:4, :], scores_ps[:, 0:512].rearrange("p (a b) -> p a b", a=4)).then_inc(fv_ready, 1)
                copy(fv[0:64, 4, :], scores_ps[0:64, 512:640]).then_inc(fv_ready, 1)

            def fox_pair(q, att, i=None, dp=0):
                for c in range(3 * KT):
                    if c % 8 == 0 and q is not None:
                        ahead.upto(U_FOX + 6 * q + c // 8 + 2, i, 6 * dp)
                    if att is None and c <= KT + 4:
                        swa_part(c, PAIRS - 1)
                    if att is not None:
                        if c == 0:
                            fox_queries(att, i, dp)
                        if c == 2:
                            fox_values(att, i, dp)
                        for j in FOX_SLOTS.get(c, ()) if c != 46 else (SLOTS,):
                            attend("fox", j, PAIRS + att, i, dp)
                    if q is not None:
                        if c == 17:
                            act.wait_ge(tile_done, lin(T_FOX + 3 * q + 1, i, 3 * dp))
                            if q:
                                act.wait_ge(v_out, lin(16 * q, i, 16 * dp))
                            copy(halves(v_t[:, :]), tile_ps(T_FOX + 3 * q)).then_inc(tile_free[(T_FOX + 3 * q) % 2], 1)
                        if c == 33:
                            act.wait_ge(tile_done, lin(T_FOX + 3 * q + 2, i, 3 * dp))
                            if q:
                                act.wait_ge(k_out, lin(16 * q, i, 16 * dp))
                            copy(halves(k_t[:, :]), tile_ps(T_FOX + 3 * q + 1))\
                                .then_inc(tile_free[(T_FOX + 3 * q + 1) % 2], 1)
                            wait_freed(act, T_FOX + 3 * q + 1, i, 3 * dp)
                            own(fk1, (k_t[0:64, :], k_t[64:128, :]), TOK)
                        if c == 34:
                            act.wait_ge(ck_landed, lin(16 * q + 16, i, 16 * dp))
                            own(fc1, (c_t[0:64, :], c_t[64:128, :]), PAST)

            fox_pair(0, None)
            with act.Fori(0, 3) as i:
                for j in range(2):
                    fox_pair(1 + j, j, i, 2)
            ahead.leave(3, 12)
            fox_pair(7, 6)

            fox_queries(7)
            act.wait_ge(out_free, 1 + 2 * (2 * PAIRS - 1))
            for c in range(KT + 2):
                k = c - 2
                if c < KT - 1:
                    act.wait_ge(y_sum, c + 1)
                    copy(x_hi[:, c, :], acc[:, c, :]).then_inc(x_hi_done, 1)
                if k >= 0:
                    if k % 4 == 0:
                        ahead.upto(U_O + k // 4 + 2)
                    if k == 2:
                        fox_values(7)
                    for j in LAST_SLOTS.get(k, ()):
                        attend("fox", j, 2 * PAIRS - 1)
            attend("fox", SLOTS, 2 * PAIRS - 1)
            act.wait_ge(out_free, 1 + 4 * PAIRS)
            act.wait_ge(y_sum, KT)
            copy(x_hi[:, KT - 1, :], acc[:, KT - 1, :]).then_inc(x_hi_done, 1)
            act.wait_ge(y_ready, KT)
            ln_square(1, 0, acc[:, 0, :])
            with act.Fori(0, 7) as i:
                for j in range(2):
                    ahead.upto(U_O + 4 + 2 * j + 3, i, 4)
                    act.wait_ge(ln_cent, i * 2 + (KT + j + 2))
                    act.wait_ge(ln_s2, i * 2 + (KT + j + 2))
                    nc.scalar.activation(WK, feature_tile(acc, i * 2 + (j + 1)), ACT.Square).then_inc(ln_sq, 1)
            ahead.leave(7, 4)
            ln_square(1, 15, acc[:, 15, :])
            ln_root(1)
            ln_apply(1, 2, acc, True, U_MLP)

            def hidden(n, m, i=None, dn=0, dm=0):
                act.wait_ge(tile_done, lin(n + 1, i, dn))
                act.wait_ge(hsq_done, lin(m + 1, i, dm))
                nc.scalar.activation(halves(WK), tile_ps(n), ACT.Relu).then_inc(tile_free[n % 2], 1)

            def hidden_hi(m, i=None, dm=0):
                act.wait_ge(hsq_done, lin(m + 2, i, dm))
                copy(hid_hi[:, m // 4 % 2, m % 4, :], WK2).then_inc(hid_hi_done, 1)

            def up(n, u, m, i=None, dn=0, du=0, dm=0):
                for k in range(4):
                    ahead.upto(u + 2 * k + 3, i, du)
                    hidden(n + k, m + k, i, dn, dm)
                    hidden_hi(m + k, i, dm)

            def down(u, i=None, du=0):
                for k in range(8):
                    ahead.upto(u + k + 2, i, du)

            act.wait_ge(ln_scaled, 2 + KT)
            act.wait_ge(x_ready, 2 + 3 * KT)
            ahead.upto(U_MLP + 9)
            up(T_MLP, U_MLP, 0)
            act.wait_ge(p_landed, 16)
            copy(p_hi[:, :, :], p_raw[:, :, :]).then_inc(p_hi_done, 1)
            with act.Fori(0, 7) as i:
                for j in range(2):
                    up(T_MLP + 4 + 20 * j, U_MLP + 8 + 16 * j, 4 + 4 * j, i, 40, 32, 8)
                    down(U_MLP + 16 + 16 * j, i, 32)
            ahead.leave(7, 32)
            up(T_MLP + 284, U_MLP + 232, 60)
            down(U_MLP + 240)
            for n in range(KT):
                ahead.upto(U_MLP + 248 + n // 2 + 2)
                if n >= 1:
                    ln_square(2, n - 1, acc[:, n - 1, :])
            ln_square(2, 15, acc[:, 15, :])

            for n in range(T_PE, T_PE + KT):
                ahead.upto(U_PE + (n - T_PE) // 4 + 2)
                act.wait_ge(tile_done, n + 1)
                copy(halves(pe_out[:, n - T_PE, :]), tile_ps(n)).then_inc(tile_free[n % 2], 1)
                if n == T_PE + 8:
                    ln_root(2)
            ln_apply(2, 3, acc, False, U_PG)

            def gate_tile(n, u, i=None, dn=0, du=0):
                kt = lin(n - T_PG, i, dn)
                ahead.upto(u + 3, i, du)
                act.wait_ge(tile_done, lin(n + 1, i, dn))
                act.wait_ge(gated, lin(n - T_PG + 1, i, dn))
                bias = cols[:, 6 * KT + kt:6 * KT + kt + 1] if i is None else cols[:, bass.ds(kt + 6 * KT, 1)]
                nc.scalar.activation(halves(st[:, n % 2, :]), tile_ps(n), ACT.Sigmoid, bias=bias)\
                    .then_inc(tile_free[n % 2], 1)

            ahead.upto(U_PG + 9)
            for j in range(4):
                gate_tile(T_PG + j, U_PG + 2 * j)
            with act.Fori(0, 5) as i:
                for j in range(2):
                    gate_tile(T_PG + 4 + j, U_PG + 8 + 2 * j, i, 2, 4)
            ahead.leave(5, 4)
            for j in range(14, 16):
                gate_tile(T_PG + j, U_PG + 2 * j)

        @block.vector
        def _(dve):
            chain = Chain(dve, ch_dve)
            V = nc.vector

            def split(u, i, du):
                dve.wait_ge(w_hi_done, lin(u + 1, i, du))
                V.tensor_tensor(w_lo[:, u % RING, :], w_raw[:, u % RING, :], w_hi[:, u % RING, :], ALU.subtract)\
                    .then_inc(w_split, 1)
            ahead = Ahead(split)

            def ln_take_shift(L):
                dve.wait_ge(ln_mm, 2 * L + 1)
                chain.add(V.tensor_scalar(halves(SH), misc_halves(0), float(KT), None, ALU.mult))
                chain.wait()

            def ln_center(tile):
                V.tensor_tensor(tile, tile, SH, ALU.subtract).then_inc(ln_cent, 1)

            def ln_add(c, i=None):
                dve.wait_ge(ln_sq, lin(c + 1, i, 2))
                dve.wait_ge(ln_s2, lin(c + 1, i, 2))
                V.tensor_tensor(S2, S2, WK, ALU.add).then_inc(ln_s2, 1)

            def ln_finish(L):
                dve.wait_ge(ln_mm, 2 * L + 2)
                chain.add(V.tensor_copy(halves(MU), misc_halves(0)))
                chain.wait()
                chain.add(V.scalar_tensor_tensor(VAR, MU, -1.0, MU, ALU.mult, ALU.mult))
                chain.wait()
                V.scalar_tensor_tensor(halves(VAR), halves(VAR), EPS, misc_halves(1024), ALU.add, ALU.add).then_inc(ln_var, 1)
                dve.wait_ge(ln_sd, L + 1)
                chain.add(V.scalar_tensor_tensor(WK2, RSTD, -0.5, RSTD, ALU.mult, ALU.mult))
                chain.wait()
                chain.add(V.tensor_tensor(WK2, WK2, VAR, ALU.mult))
                chain.wait()
                V.scalar_tensor_tensor(RSTD, WK2, 1.5, RSTD, ALU.add, ALU.mult).then_inc(ln_rstd, 1)

            def ln_apply(L, gen, src, u):
                dve.wait_ge(ln_rstd, L + 1)
                for c in range(KT + 2):
                    if c < KT:
                        if L == 1:
                            chain.add(V.tensor_tensor(src[:, c, :], src[:, c, :], MU, ALU.subtract))
                            chain.wait()
                        else:
                            dve.wait_ge(ln_sub, KT * (L // 2) + c + 1)
                        V.tensor_tensor(src[:, c, :], src[:, c, :], RSTD, ALU.mult).then_inc(ln_mul, 1)
                    if c >= 2:
                        k = c - 2
                        if k % 2 == 0:
                            ahead.upto(u + 1 + k // 2)
                        dve.wait_ge(x_hi_done, KT * gen + k + 1)
                        V.tensor_tensor(x_lo[:, k, :], st[:, 3 + k % 2, :], x_hi[:, k, :], ALU.subtract).then_inc(x_ready, 1)

            def attend(kind, j, pair, i=None, dp=0):
                g0, dg = STEPS * pair, STEPS * dp
                p = s_p if kind == "swa" else f_p
                if j < STEPS:
                    dve.wait_ge(scored, lin(g0 + j + 1, i, dg))
                    at, width = span(kind, j)
                    V.reduce_max(stat[:, j % 3, 0:1], scores_ps[:, at:at + width], AX, negate=True).then_inc(negmax, 1)
                if 1 <= j <= STEPS:
                    s = (j - 1) % 3
                    dve.wait_ge(exp_done, lin(g0 + j + 2, i, dg))
                    at, width = span(kind, j - 1)
                    chain.add(V.reciprocal(stat[:, s, 2:3], stat[:, s, 1:2]))
                    chain.wait()
                    row = p[:, (j - 1) % 4, 0:width]
                    V.tensor_scalar(row, row, stat[:, s, 2:3], None, ALU.mult)\
                        .then_inc(normed, 1)

            dve.sem_inc(w_split, RING)
            dve.sem_inc(tile_free[0], 2)
            dve.sem_inc(tile_free[1], 2)
            dve.sem_inc(hsq_done, 1)
            dve.sem_inc(x_ready, 2)
            dve.sem_inc(gated, 2)
            chain.add(V.memset(S2, 0.0))
            V.memset(mean_w[:, :], 1.0 / D).then_inc(zeroed_v, 1)
            chain.wait()
            dve.sem_inc(ln_s2, 1)
            dve.wait_ge(x_landed[0], 16)
            ln_take_shift(0)
            for c in range(KT):
                if c % 4 == 0:
                    dve.wait_ge(x_landed[c // 4], 16)
                ln_center(acc[:, c, :])
                if c >= 1:
                    ln_add(c - 1)
            ln_add(15)
            ahead.upto(1)
            ln_finish(0)
            ln_apply(0, 0, acc, U_KV)

            def lows(pairs, count, i=None, dc=0):
                for (dst, src, hi, scale), k in zip(pairs, range(len(pairs))):
                    dve.wait_ge(op_act, lin(count + k + 1, i, dc))
                    ins = V.scalar_tensor_tensor(dst, src, scale, hi, ALU.mult, ALU.subtract).then_inc(op_dve, 1)
                return ins

            cc = slice(CACHE_COL, CACHE_COL + WIN)
            lows([(sk2[0:64, 0, cc], ck_t[0:64, :], sk1[0:64, 0, cc], 1.0),
                  (sk2[64:128, 1, cc], ck_t[64:128, :], sk1[64:128, 1, cc], 1.0)], 0)

            def rotate(r, n, i=None, dr=0):
                out, free = (k_rot, keys_out) if n == T_KV else (rot, tile_free[n % 2])
                dve.wait_ge(swapped, lin(r + 1, i, dr))
                V.tensor_tensor(halves(rot2[:, :]), tile_ps(n), halves(sin_t[:, :]), ALU.mult).then_inc(free, 1)
                dve.wait_ge(cos_done, lin(r + 1, i, dr))
                if n == T_KV:
                    dve.wait_ge(keys_out, 1)
                else:
                    wait_freed(dve, n, i, dr)
                V.tensor_tensor(out[:, :], out[:, :], rot2[:, :], ALU.add).then_inc(rot_ready, 1)
                dve.wait_ge(rot_ready, lin(r + 1, i, dr))

            def row(col, n=TOK):
                return f_tmp[:, col:col + n]

            def rounded(col):
                return f_tmp.bitcast(f32r)[:, col:col + F_ALL]
            dve.wait_ge(tile_done, 3)
            dve.wait_ge(ln_h, KT)
            V.tensor_scalar(halves(row(F_D)), tile_ps(2)[0:16], bf[:, :], None, ALU.add).then_inc(tile_free[0], 1)
            ahead.upto(U_KV + 9)
            rotate(0, T_KV)
            lows([(sk2[0:64, 0, 0:TOK], k_rot[0:64, :], sk1[0:64, 0, 0:TOK], 1.0),
                  (sk2[64:128, 1, 0:TOK], k_rot[64:128, :], sk1[64:128, 1, 0:TOK], 1.0)], 2)

            def gates(c):
                if c == 5:
                    wait_freed(dve, 2)
                    V.scalar_tensor_tensor(row(F_X), row(F_D), -1.0, row(F_D), ALU.mult, ALU.max).then_inc(f_arg, 1)
                    chain.add(V.tensor_scalar(row(F_M), row(F_D), 0.0, None, ALU.min))
                if c == 7:
                    dve.wait_ge(f_exp, 1)
                    V.tensor_scalar(row(F_W), row(F_E), 1.0, None, ALU.add).then_inc(f_w, 1)
                    dve.wait_ge(f_w, 1)
                    chain.wait()
                    chain.add(V.tensor_scalar(row(F_D), row(F_W), -1.0, None, ALU.add))
                    chain.wait()
                    chain.add(V.tensor_scalar(row(F_R), row(F_D), 2.0 ** -23, None, ALU.max))
                if c == 9:
                    chain.wait()
                    chain.add(V.reciprocal(row(F_R), row(F_R)))
                if c == 10:
                    chain.wait()
                    chain.add(V.tensor_tensor(row(F_R), row(F_R), row(F_E), ALU.mult))
                    chain.wait()
                    dve.wait_ge(f_log, 1)
                    chain.add(V.tensor_tensor(row(F_L), row(F_L), row(F_R), ALU.mult))
                    chain.add(V.scalar_tensor_tensor(row(F_D), row(F_D), 0.0, row(F_E), ALU.is_equal, ALU.mult))
                if c == 11:
                    chain.wait()
                    chain.add(V.tensor_tensor(row(F_L), row(F_L), row(F_D), ALU.add))
                    chain.wait()
                    chain.add(V.tensor_tensor(row(F_G), row(F_M), row(F_L), ALU.subtract))
                    chain.add(V.memset(row(F_X), 0.0))
                if c == 13:
                    chain.wait()
                    dve.wait_ge(clogf_landed, 16)
                    chain.add(V.tensor_tensor_scan(row(F_SUM, PROMPT), row(F_X, PROMPT), row(F_G, PROMPT), 0.0, ALU.add, ALU.add))
                    chain.add(V.tensor_tensor_scan(row(F_SUM + TOK, PAST), row(F_X, PAST), row(F_C, PAST), 0.0, ALU.add, ALU.add))
                    chain.wait()
                    last = F_SUM + TOK + PAST - 1
                    V.tensor_tensor_scan(row(F_SUM + PROMPT, SAMPLE), row(F_X, SAMPLE), row(F_G + PROMPT, SAMPLE),
                                         row(last, 1), ALU.add, ALU.add).then_inc(f_sum, 1)
                if c == 15:
                    dve.wait_ge(f_hi, 1)
                    V.tensor_tensor(rounded(F_LO), row(F_SUM, F_ALL), row(F_HI, F_ALL), ALU.subtract).then_inc(f_rows, 1)
                    V.tensor_scalar(rounded(F_NHI), row(F_HI, F_ALL), -1.0, None, ALU.mult).then_inc(f_rows, 1)
                    dve.wait_ge(f_rows, 2)
                    V.tensor_scalar(rounded(F_NLO), row(F_LO, F_ALL), -1.0, None, ALU.mult).then_inc(f_rows, 1)
                    V.memset(row(F_ONE), 1.0).then_inc(f_rows, 1)

            def swa_part(c, att, i=None, dp=0):
                if c == 2:
                    rotate(att + 1, T_QA + att, i, dp)
                    lows([(sq1[64:128, 0, :], rot[0:64, :], sq1[0:64, 0, :], SCALE),
                          (sq1[0:64, 1, :], rot[64:128, :], sq1[64:128, 1, :], SCALE)], OP_KV + 2 * att, i, 2 * dp)
                if KT + c in SWA_SLOTS and att:
                    attend("swa", SWA_SLOTS[KT + c], att - 1, i, dp)
                if c in SWA_SLOTS:
                    attend("swa", SWA_SLOTS[c], att, i, dp)

            def swa_pair(q, att, i=None, dp=0):
                for c in range(KT):
                    if c % 8 == 0:
                        ahead.upto(U_QA + 2 * q + c // 8 + 2, i, 2 * dp)
                    swa_part(c, att, i, dp)
                    if q == 1:
                        gates(c)

            swa_pair(1, 0)
            with dve.Fori(0, 3) as i:
                chain.enter(i, 2 * STEPS)
                for j in range(2):
                    swa_pair(2 + j, 1 + j, i, 2)
                chain.leave(3)
            ahead.leave(3, 4)

            def fox_queries(att, i=None, dp=0):
                n = T_FOX + 3 * att + 2
                ps = tile_ps(n)
                lows([(halves(fq1[64:128, 0, :]), ps[0:64], halves(fq1[0:64, 0, :]), SCALE),
                      (halves(fq1[0:64, 1, :]), ps[64:128], halves(fq1[64:128, 1, :]), SCALE)],
                     OP_FOX_A + 6 * att + 4, i, 6 * dp)
                dve.wait_ge(op_dve, lin(OP_FOX_A + 6 * att + 6, i, 6 * dp))
                dve.sem_inc(tile_free[n % 2], 1)

            def fox_pair(q, att, i=None, dp=0):
                n0, dn, df = T_FOX + 3 * (q or 0), 3 * dp, 6 * dp
                for c in range(3 * KT):
                    if c % 8 == 0 and q is not None:
                        ahead.upto(U_FOX + 6 * q + c // 8 + 2, i, 6 * dp)
                    if att is None and c <= KT + 4:
                        swa_part(c, PAIRS - 1)
                    if att is not None:
                        if c == 0:
                            fox_queries(att, i, dp)
                        for j in FOX_SLOTS.get(c, ()):
                            attend("fox", j, PAIRS + att, i, dp)
                    if q is not None:
                        if c == 33:
                            wait_freed(dve, n0 + 1, i, dn)
                            lows([(fk2[0:64, 0, :], k_t[0:64, :], fk1[0:64, 0, :], 1.0),
                                  (fk2[64:128, 1, :], k_t[64:128, :], fk1[64:128, 1, :], 1.0)], OP_FOX_A + 6 * q, i, df)
                        if c == 34:
                            lows([(fc2[0:64, 0, :], c_t[0:64, :], fc1[0:64, 0, :], 1.0),
                                  (fc2[64:128, 1, :], c_t[64:128, :], fc1[64:128, 1, :], 1.0)], OP_FOX_A + 6 * q + 2, i, df)

            fox_pair(0, None)
            with dve.Fori(0, 3) as i:
                chain.enter(i, 2 * STEPS)
                for j in range(2):
                    fox_pair(1 + j, j, i, 2)
                chain.leave(3)
            ahead.leave(3, 12)
            fox_pair(7, 6)

            fox_queries(7)
            chain.add(V.memset(S2, 0.0))
            dve.wait_ge(tile_done, T_O)

            def operand_low(c):
                dve.wait_ge(x_hi_done, KT + c + 1)
                V.tensor_tensor(x_lo[:, c, :], acc[:, c, :], x_hi[:, c, :], ALU.subtract).then_inc(x_ready, 1)
            for c in range(KT + 3):
                k = c - 3
                if c < KT:
                    if c >= 3:
                        dve.wait_ge(y_ready, c - 2)
                    V.tensor_tensor(st[:, 2 + c % 3, :], x_hi[:, c, :], x_lo[:, c, :], ALU.add).then_inc(y_sum, 1)
                    if c >= 1:
                        operand_low(c - 1)
                if k >= 0:
                    if k % 4 == 0:
                        ahead.upto(U_O + k // 4 + 2)
                    for j in LAST_SLOTS.get(k, ()):
                        attend("fox", j, 2 * PAIRS - 1)
            operand_low(KT - 1)

            def residual(dst, n, i=None, dn=0):
                dve.wait_ge(tile_done, lin(n + 1, i, dn))
                d = feature_tile(acc, lin(n - T_O, i, dn)) if dst is None else dst
                if dst is None:
                    V.scalar_tensor_tensor(halves(d), halves(d), ALPHA, tile_ps(n), ALU.mult, ALU.add).then_inc(tile_free[n % 2], 1)
                else:
                    V.tensor_tensor(halves(d), halves(d), tile_ps(n), ALU.add).then_inc(tile_free[n % 2], 1)

            for n in range(T_O, T_O + 2):
                ahead.upto(U_O + 2 * (n - T_O) + 3)
                dve.wait_ge(y_ready, n - T_O + 1)
                residual(None, n)
            dve.wait_ge(y_ready, KT)
            ln_take_shift(1)
            wait_freed(dve, T_O)
            ln_center(acc[:, 0, :])
            with dve.Fori(0, 7) as i:
                for j in range(2):
                    ahead.upto(U_O + 4 + 2 * j + 3, i, 4)
                    dve.wait_ge(y_ready, i * 2 + (j + 3))
                    residual(None, T_O + 2 + j, i, 2)
                    wait_freed(dve, T_O + 1 + j, i, 2)
                    ln_center(feature_tile(acc, i * 2 + (j + 1)))
                    ln_add(KT + j, i)
            ahead.leave(7, 4)
            wait_freed(dve, T_O + 15)
            ln_center(acc[:, 15, :])
            ln_add(KT + 14)
            ln_add(KT + 15)
            ln_finish(1)
            ln_apply(1, 2, acc, U_MLP)

            def hidden(n, m, i=None, dn=0, dm=0):
                wait_freed(dve, n, i, dn)
                dve.wait_ge(hid_ready, lin(m, i, dm)) if m or i is not None else None
                V.tensor_tensor(WK2, WK, WK, ALU.mult).then_inc(hsq_done, 1)
                dve.wait_ge(hid_hi_done, lin(m + 1, i, dm))
                V.tensor_tensor(hid_lo[:, m // 4 % 2, m % 4, :], WK2, hid_hi[:, m // 4 % 2, m % 4, :], ALU.subtract)\
                    .then_inc(hid_ready, 1)

            def up(n, u, m, i=None, dn=0, du=0, dm=0):
                for k in range(4):
                    ahead.upto(u + 2 * k + 3, i, du)
                    hidden(n + k, m + k, i, dn, dm)

            def down(n, u, i=None, dn=0, du=0):
                for k in range(KT):
                    ahead.upto(u + k // 2 + 2, i, du)
                    residual(acc[:, k, :], n + k, i, dn)

            dve.wait_ge(ln_scaled, 2 + KT)
            ahead.upto(U_MLP + 9)
            up(T_MLP, U_MLP, 0)
            dve.wait_ge(p_hi_done, 1)
            V.tensor_tensor(p_lo[:, :, :], p_raw[:, :, :], p_hi[:, :, :], ALU.subtract).then_inc(p_ready, 1)
            dve.wait_ge(ln_scaled, 2 + KT)
            with dve.Fori(0, 7) as i:
                for j in range(2):
                    up(T_MLP + 4 + 20 * j, U_MLP + 8 + 16 * j, 4 + 4 * j, i, 40, 32, 8)
                    down(T_MLP + 8 + 20 * j, U_MLP + 16 + 16 * j, i, 40, 32)
            ahead.leave(7, 32)
            up(T_MLP + 284, U_MLP + 232, 60)
            down(T_MLP + 288, U_MLP + 240)
            chain.add(V.memset(S2, 0.0))
            for c in range(KT):
                n = T_MLP + 304 + c
                ahead.upto(U_MLP + 248 + c // 2 + 2)
                residual(acc[:, c, :], n)
                if c == 1:
                    ln_take_shift(2)
                if c >= 1:
                    wait_freed(dve, n - 1)
                    ln_center(acc[:, c - 1, :])
                if c >= 2:
                    ln_add(2 * KT + c - 2)
            wait_freed(dve, T_MLP + 319)
            ln_center(acc[:, 15, :])
            ln_add(2 * KT + 14)
            ln_add(2 * KT + 15)
            for u in range(U_PE, U_PE + 4):
                ahead.upto(u + 2)
                if u == U_PE + 1:
                    ln_finish(2)
            ln_apply(2, 3, acc, U_PG)

            def gate_tile(n, u, i=None, dn=0, du=0):
                kt = lin(n - T_PG, i, dn)
                d = st[:, 2 + n % 2, :]
                ahead.upto(u + 3, i, du)
                g = st[:, n % 2, :]
                if i is not None or n >= T_PG + 2:
                    dve.wait_ge(y_out[n % 2], lin(16 * ((n - T_PG) // 2), i, 16))
                chain.add(V.tensor_tensor(d, feature_tile(x_hi, kt), feature_tile(x_lo, kt), ALU.add))
                wait_freed(dve, n, i, dn)
                chain.add(V.tensor_tensor(g, g, feature_tile(pe_out, kt), ALU.mult))
                chain.wait()
                V.tensor_tensor(d, d, g, ALU.add).then_inc(gated, 1)

            dve.wait_ge(x_ready, 2 + 4 * KT)
            ahead.upto(U_PG + 9)
            for j in range(4):
                gate_tile(T_PG + j, U_PG + 2 * j)
            with dve.Fori(0, 5) as i:
                chain.enter(i, 4)
                for j in range(2):
                    gate_tile(T_PG + 4 + j, U_PG + 8 + 2 * j, i, 2, 4)
                chain.leave(5)
            ahead.leave(5, 4)
            for j in range(14, 16):
                gate_tile(T_PG + j, U_PG + 2 * j)

        @block.gpsimd
        def _(pool):
            P = nc.gpsimd

            def ln_sum(L, src):
                P.memset(S1, 0.0).then_inc(ch_pool, 1)
                pool.wait_ge(ch_pool, L + 1)
                with pool.Fori(0, KT) as i:
                    pool.wait_ge(ln_cent, i + (KT * L + 1))
                    pool.wait_ge(ln_s1, i + (KT * L + 1))
                    P.tensor_tensor(S1, S1, feature_tile(src, i), ALU.add).then_inc(ln_s1, 1)

            def ln_sub_mean(L, src, scaled):
                pool.wait_ge(ln_var, L + 1)

                def sub(kt):
                    s = feature_tile(src, kt)
                    P.tensor_tensor(s, s, MU, ALU.subtract).then_inc(ln_sub, 1)

                def scale(kt, c):
                    pool.wait_ge(ln_h, KT * L + c + 1)
                    P.tensor_scalar(feature_tile(acc, kt), st[:, 3 + c % 2, :], ALPHA, None, ALU.mult).then_inc(ln_scaled, 1)
                if scaled:
                    for kt in range(KT):
                        scale(kt, kt)
                else:
                    with pool.Fori(0, KT) as i:
                        sub(i)

            def pool_count(count):
                return count if count < OP_FOX_A else count - OP_FOX_A + OP_FOX_P

            def lanes_free(sem_, count, i=None, step=0):
                pool.wait_ge(sem_, lin(count, i, step))

            def duplicate(parts, count, i=None, dc=0):
                for k, (d, s) in enumerate(parts):
                    pool.wait_ge(op_act, lin(count + k + 1, i, dc))
                    if k or count:
                        pool.wait_ge(op_pool, lin(pool_count(count) + k, i, dc))
                    if i is not None:
                        settle(pool)
                    P.tensor_copy(d, s).then_inc(op_pool, 1)

            pool.sem_inc(turned, 2)
            pool.sem_inc(weighed, 2)
            pool.sem_inc(units_begun, 3)
            pool.sem_inc(ln_scaled, 2)
            pool.sem_inc(ln_s1, 1)
            ln_sum(0, acc)
            lanes_free(ln_s1, 1 + KT)
            for k, z in enumerate((sk2[64:128, 0, :].bitcast(f32), sk2[0:64, 1, :].bitcast(f32))):
                P.memset(z, 0.0).then_inc(zeroed_p, 1)
                lanes_free(zeroed_p, k + 1)
            ln_sub_mean(0, acc, False)
            lanes_free(ln_sub, KT)
            cc = slice(CACHE_COL, CACHE_COL + WIN)
            duplicate([(sk1[64:128, 0, cc], sk1[0:64, 0, cc]), (sk1[0:64, 1, cc], sk1[64:128, 1, cc])], 0)
            lanes_free(op_pool, 2)
            pool.wait_ge(ln_h, KT)
            pool.dma_start(f_row(F_C, PAST), t["clogf"]).then_inc(clogf_landed, 16)

            def cosine(r, i=None, dr=0):
                pool.wait_ge(z_ready, lin(r + 1, i, dr))
                P.tensor_tensor((rot if r else k_rot)[:, :], z_t[:, :], cos_t[:, :], ALU.mult).then_inc(cos_done, 1)
            cosine(0)
            lanes_free(cos_done, 1)
            kk = slice(0, TOK)
            duplicate([(sk1[64:128, 0, kk], sk1[0:64, 0, kk]), (sk1[0:64, 1, kk], sk1[64:128, 1, kk])], 2)
            lanes_free(op_pool, OP_KV)
            pool.wait_ge(rot_ready, 1)
            cosine(1)
            pool.wait_ge(va_out, 1)
            for new, cached, name in ((k_rot, ck_t, "swa_k"), (va_t, cv_t, "swa_v")):
                pool.dma_start(t[name + "_p"], new[:, PROMPT - WIN:PROMPT]).then_inc(kv_out, 16)
                pool.dma_start(t[name + "_s"][:, 0:WIN - SAMPLE], cached[:, SAMPLE:WIN]).then_inc(kv_out, 16)
                pool.dma_start(t[name + "_s"][:, WIN - SAMPLE:WIN], new[:, PROMPT:TOK]).then_inc(kv_out, 16)
            pool.wait_ge(f_rows, 4)
            pool.dma_start(t["logf"], f_row(F_G, TOK)).then_inc(f_saved, 16)
            for k, (q, kk_, cc_) in enumerate(((F_HI, F_ONE, F_ONE), (F_LO, F_ONE, F_ONE), (F_ONE, F_NHI, F_NHI), (F_ONE, F_NLO, F_NLO))):
                pool.dma_start(t["rows_q"][:, k, :], f_row(q, TOK)).then_inc(f_saved, 16)
                pool.dma_start(t["rows_k"][:, k, :], f_row(kk_, TOK)).then_inc(f_saved, 16)
                pool.dma_start(t["rows_c"][:, k, :], f_row(cc_ if cc_ == F_ONE else cc_ + TOK, PAST)).then_inc(f_saved, 16)
            pool.wait_ge(kv_out, 96)
            pool.wait_ge(f_saved, 16 * 13)

            def cosine_after(r, i=None, dr=0):
                pool.wait_ge(op_dve, lin(OP_KV + 2 * r - 2, i, 2 * dr))
                cosine(r, i, dr)
            with pool.Fori(0, 7) as i:
                cosine_after(2, i, 1)

            def zeros(first, parts):
                for k, z in enumerate(parts):
                    P.memset(z, 0.0).then_inc(zeroed_p, 1)
                    lanes_free(zeroed_p, first + k + 1)

            def other_halves(m):
                return m[64:128, 0, :].bitcast(f32), m[0:64, 1, :].bitcast(f32)
            pool.wait_ge(op_dve, OP_KV + 2 * PAIRS)
            zeros(ZERO_SWA, (*other_halves(fk2), *other_halves(fc2)))

            def fox_pair(q, att, i=None, dp=0):
                dn, df = 3 * dp, 6 * dp

                def dram(tensor, index, n, step):
                    return tensor[index:index + n] if i is None else tensor[bass.ds(i * step + index, n)]
                if att is not None:
                    duplicate([(fq2[0:64, 0, :], fq1[0:64, 0, :]), (fq2[64:128, 1, :], fq1[64:128, 1, :])],
                              OP_FOX_A + 6 * att + 4, i, df)
                    pool.wait_ge(weighed, lin(2 + STEPS * (PAIRS + att), i, STEPS * dp))
                    if i is not None:
                        settle(pool)
                    pool.dma_start(c_v[:, :, :], dram(t["cv"], att, 1, dp).rearrange("o p k c -> p (o k) c")).then_inc(cv_landed, 16)
                if q is None:
                    return
                if q or i is not None:
                    pool.wait_ge(op_dve, lin(OP_FOX_A + 6 * q - 2, i, df))
                if i is not None:
                    settle(pool)
                pool.dma_start(c_t[:, :], dram(t["ck"], q, 1, dp).rearrange("o p c -> p (o c)")).then_inc(ck_landed, 16)
                wait_freed(pool, T_FOX + 3 * q, i, dn)
                if i is not None:
                    settle(pool)
                pool.dma_start(dram(t["fox_v"], q, 1, dp).rearrange("o p c -> p (o c)"), v_t[:, :]).then_inc(v_out, 16)
                pool.wait_ge(scored, lin(STEPS * (PAIRS + q), i, STEPS * dp))
                if i is not None:
                    settle(pool)
                if q == 0:
                    pool.wait_ge(out_free, 1 + 2 * PAIRS)
                    pool.wait_ge(weighed, 2 + STEPS * PAIRS)
                    zeros(ZERO_SWA + 4, other_halves(fq2))
                for dst, name in ((fq2, "rows_q"), (fk2, "rows_k"), (fc2, "rows_c")):
                    for head, at in ((0, 64), (1, 0)):
                        pool.dma_start(dst[at:at + 4, head, :].bitcast(f32),
                                       dram(t[name], 2 * q + head, 1, 2 * dp).rearrange("o r c -> (o r) c"))\
                            .then_inc(forget_rows, 16)
                wait_freed(pool, T_FOX + 3 * q + 1, i, dn)
                if i is not None:
                    settle(pool)
                pool.dma_start(dram(t["fox_k"], q, 1, dp).rearrange("o p c -> p (o c)"), k_t[:, :]).then_inc(k_out, 16)
                duplicate([(fk1[64:128, 0, :], fk1[0:64, 0, :]), (fk1[0:64, 1, :], fk1[64:128, 1, :])],
                          OP_FOX_A + 6 * q, i, df)
                duplicate([(fc1[64:128, 0, :], fc1[0:64, 0, :]), (fc1[0:64, 1, :], fc1[64:128, 1, :])],
                          OP_FOX_A + 6 * q + 2, i, df)

            fox_pair(0, None)
            with pool.Fori(0, 3) as i:
                for j in range(2):
                    fox_pair(1 + j, j, i, 2)
            fox_pair(7, 6)
            fox_pair(None, 7)

            lanes_free(op_pool, OP_FOX_P + 6 * PAIRS)
            for c in range(KT):
                pool.wait_ge(y_sum, c + 1)
                pool.wait_ge(x_ready, 2 + KT + c + 1)
                P.tensor_copy(acc[:, c, :], st[:, 2 + c % 3, :]).then_inc(y_ready, 1)
            ln_sum(1, acc)
            ln_sub_mean(1, acc, True)
            pool.wait_ge(ln_mul, 2 * KT)
            pool.dma_start(p_raw[:, :, :], t["p"]).then_inc(p_landed, 16)
            pool.wait_ge(hid_ready, 64)
            ln_sum(2, acc)
            ln_sub_mean(2, acc, False)

            with pool.Fori(0, KT // 2) as i:
                for j in range(2):
                    pool.wait_ge(gated, i * 2 + (j + 3))
                    settle(pool)
                    pool.dma_start(t["y"][bass.ds(i * 2 + j, 1)].rearrange("o p c -> p (o c)"),
                                   st[:, 2 + (T_PG + j) % 2, :]).then_inc(y_out[(T_PG + j) % 2], 16)
            pool.wait_ge(v_out, 16 * PAIRS)
            pool.wait_ge(k_out, 16 * PAIRS)
            for k in range(2):
                pool.wait_ge(y_out[k], 16 * 8)



def constants():
    import numpy as np
    half = 32
    inv = (np.float32(10000.0) ** (-np.arange(half, dtype=np.float32) / np.float32(half))).astype(np.float32)
    ang = np.arange(TOK, dtype=np.float32)[None, :] * inv[:, None]
    cos, sin = np.cos(ang).astype(np.float32), np.sin(ang).astype(np.float32)
    r = np.arange(128)
    q, k = np.meshgrid(r, np.arange(256), indexing="ij")
    out_of_window = ((q < 64) & (k >= 192)) | ((q >= 64) & (k < 64))
    return {
        "ident": np.eye(128, dtype=np.float32),
        "cos": np.concatenate([cos] * 4), "sin": np.concatenate([-sin, sin] * 2),
        "swap": np.eye(128, dtype=np.float32)[(r // 64) * 64 + (r % 64 + 32) % 64],
        "tri": np.where(r[None, :] > r[:, None], NEG, 0.0).astype(np.float32),
        "win": np.where(out_of_window, NEG, 0.0).astype(np.float32),
    }


def kernel(x_prompt, x_sample, p_prompt, p_sample, cache_swa_k, cache_swa_v, cache_fox_k, cache_fox_v, cache_fox_logf,
           ln0_g, ln0_b, w_in, b_f, sinks, w_o, ln1_g, ln1_b, w_up, w_down, ln2_g, ln2_b, w_pg, b_pg, w_pe):
    import numpy as np
    import concourse.bacc as bacc
    from concourse.bass_utils import run_bass_kernel_spmd

    def arr(a):
        return np.asarray(a)

    def units(w):
        n = w.shape[1] // 128
        return w.reshape(2, 8, 128, n, 128).transpose(3, 0, 2, 1, 4).reshape(2 * n, 128, 1024)

    def quads(w):
        return w.reshape(8, 2, 128, 512).transpose(0, 2, 1, 3).reshape(8, 128, 1024)

    def by_tile(v):
        return v.reshape(KT, 128).T

    wi = arr(w_in)[0]
    qa, ka, va, qb, kb, vb = (wi[:, a:b] for a, b in ((0, 1024), (1024, 1152), (1152, 1280), (1280, 2304), (2304, 3328), (3328, 4352)))
    qa = qa.reshape(D, 2, 8, 64).transpose(0, 2, 1, 3).reshape(D, 1024)
    fox = np.stack([units(vb).reshape(8, 2, 128, 1024), units(kb).reshape(8, 2, 128, 1024), units(qb).reshape(8, 2, 128, 1024)], 1)
    wo = arr(w_o)[0]
    wo = np.concatenate([wo[:1024].reshape(2, 8, 64, D).transpose(1, 0, 2, 3).reshape(1024, D), wo[1024:]])
    duo = wo[:, 0:256].reshape(4, 4, 128, 256).transpose(0, 2, 1, 3).reshape(4, 128, 1024)
    up = units(arr(w_up)[0]).reshape(FF_BLOCKS, 8, 128, 1024)
    down = arr(w_down)[0].reshape(FF_BLOCKS, 4, 128, 8, 256).transpose(0, 3, 2, 1, 4).reshape(FF_BLOCKS, 8, 128, 1024)
    first = np.concatenate([ka, va, wi[:, 4352:4368], np.zeros((D, 112), np.float32), qa[:, 0:128]], 1)
    up[0] = quads(arr(w_up)[0][:, 0:512])
    parts = [quads(first), units(qa[:, 128:]), fox.reshape(48, 128, 1024), duo, units(wo[:, 256:]), up[0]]
    for k in range(FF_BLOCKS):
        if k + 1 < FF_BLOCKS:
            parts.append(up[k + 1])
        parts.append(down[k])
    parts.append(arr(w_pe)[0].reshape(2, 128, 4, 512).transpose(2, 1, 0, 3).reshape(4, 128, 1024))
    parts += [quads(arr(w_pg)[0][:, 0:512]), units(arr(w_pg)[0][:, 512:])]
    stream = np.concatenate(parts)
    tokens = np.concatenate([arr(x_prompt)[0], arr(x_sample)[0]])
    emb = np.concatenate([arr(p_prompt)[0, 0], arr(p_sample)[0, 0]])
    data = {
        "x": tokens.T.reshape(KT, 128, TOK).transpose(1, 0, 2),
        "w": stream,
        "p": emb.T.reshape(2, 128, TOK).transpose(1, 0, 2),
        "cols": np.concatenate([by_tile(arr(v).reshape(-1)) for v in (ln0_g, ln0_b, ln1_g, ln1_b, ln2_g, ln2_b, b_pg)], 1),
        "sinks": np.broadcast_to(arr(sinks)[0].reshape(2, 8).T.reshape(1, 16), (128, 16)),
        "bf": arr(b_f)[0].reshape(16, 1),
        "swa_ck": arr(cache_swa_k)[0, 0].reshape(WIN, 128).T,
        "swa_cv_t": arr(cache_swa_v)[0, 0].reshape(WIN, 128).T,
        "swa_cv": arr(cache_swa_v)[0, 0].reshape(WIN, 128),
        "ck": arr(cache_fox_k)[0, 0].reshape(PAST, 8, 128).transpose(1, 2, 0),
        "cv": arr(cache_fox_v)[0, 0].reshape(4, 128, 8, 128).transpose(2, 1, 0, 3),
        "clogf": arr(cache_fox_logf)[0, 0].T,
        **constants(),
    }
    outs = {"y": (KT, 128, TOK), "swa_k_p": (128, WIN), "swa_v_p": (128, WIN), "swa_k_s": (128, WIN), "swa_v_s": (128, WIN),
            "fox_k": (8, 128, TOK), "fox_v": (8, 128, TOK), "logf": (16, TOK)}
    scratch = {"rows_q": (16, 4, TOK), "rows_k": (16, 4, TOK), "rows_c": (16, 4, PAST)}
    nc = bacc.Bacc("TRN2", target_bir_lowering=False, num_devices=1, dynamic_dma_scratch_size=4096)
    f32 = mybir.dt.float32
    data = {f"in_{k}": np.ascontiguousarray(v) for k, v in data.items()}
    t = {k[3:]: nc.dram_tensor(k, v.shape, f32, kind="ExternalInput").ap() for k, v in data.items()}
    t.update({k: nc.dram_tensor(f"out_{k}", v, f32, kind="ExternalOutput").ap() for k, v in outs.items()})
    t.update({k: nc.dram_tensor(k, v, f32, kind="Internal").ap() for k, v in scratch.items()})
    build(nc, t)
    r = run_bass_kernel_spmd(nc, [data], core_ids=[0]).results[0]
    o = {k: r[f"out_{k}"] for k in outs}

    def rows(a, lo, hi):
        return a.reshape(-1, a.shape[-1])[:, lo:hi].T

    def heads(a, lo, hi, n):
        return np.ascontiguousarray(rows(a, lo, hi)).reshape(1, 1, hi - lo, n, 64)

    yt = rows(o["y"], 0, TOK)
    lf = rows(o["logf"], 0, TOK)
    return (np.ascontiguousarray(yt[:PROMPT])[None], np.ascontiguousarray(yt[PROMPT:])[None],
            heads(o["swa_k_p"], 0, WIN, 2), heads(o["swa_v_p"], 0, WIN, 2),
            heads(o["fox_k"], 0, PROMPT, 16), heads(o["fox_v"], 0, PROMPT, 16), np.ascontiguousarray(lf[:PROMPT])[None, None],
            heads(o["swa_k_s"], 0, WIN, 2), heads(o["swa_v_s"], 0, WIN, 2),
            heads(o["fox_k"], PROMPT, TOK, 16), heads(o["fox_v"], PROMPT, TOK, 16), np.ascontiguousarray(lf[PROMPT:])[None, None])
```
